# Optimizing a Trainium2 kernel written in Bass

```python
import math
import jax, jax.numpy as jnp
from jax import lax
import numpy as np

D_MODEL = 1024
BATCH = 1
SEQ = 2048
DEPTH = 1

CTX_LEN = 256
GRID_W = 64

W_LRU = D_MODEL // 2
W_POOL = D_MODEL // 4
W_CONF = D_MODEL // 4
W_MIX = W_LRU + W_POOL + W_CONF

LRU_HEADS = 8
LRU_HD = W_LRU // LRU_HEADS
LRU_CONV = 4
LRU_C = 8.0

POOL_WINDOWS = (2, 4, 8, 16)
POOL_GROUPS = len(POOL_WINDOWS)
POOL_GD = W_POOL // POOL_GROUPS

CONF_K = 31

IN_WIDTHS = (W_LRU, W_LRU, W_POOL, W_POOL, W_CONF, W_CONF, W_CONF)
N_IN = sum(IN_WIDTHS)
IN_SPLITS = tuple(int(v) for v in np.cumsum(IN_WIDTHS)[:-1])

EPS = 1e-6
LN_EPS = 1e-5

kernel_name = "hybrid_lru_pool_conformer_dit"

def rmsnorm(x, g):
    x32 = x.astype(jnp.float32)
    y = x32 * lax.rsqrt(jnp.mean(x32 * x32, axis=-1, keepdims=True) + EPS)
    return (y * g.astype(jnp.float32)).astype(x.dtype)

def pos_embed_2d(n):
    ROWS = n // GRID_W
    row = jnp.repeat(jnp.arange(ROWS, dtype=jnp.float32), GRID_W)
    col = jnp.tile(jnp.arange(GRID_W, dtype=jnp.float32), ROWS)
    q = D_MODEL // 4
    omega = 1.0 / (10000.0 ** (jnp.arange(q, dtype=jnp.float32) / q))
    def enc(p):
        ang = p[:, None] * omega[None, :]
        return jnp.concatenate([jnp.sin(ang), jnp.cos(ang)], axis=-1)
    return jnp.concatenate([enc(row), enc(col)], axis=-1)

def modulation(cond, w_mod, b_mod):
    m = jnp.dot(jax.nn.silu(cond), w_mod) + b_mod
    return jnp.split(m, 3, axis=-1)

def dwconv(x, w, b, pad_l, pad_r):
    C = x.shape[-1]
    y = lax.conv_general_dilated(
        x, w[:, None, :].astype(x.dtype), window_strides=(1,), padding=[(pad_l, pad_r)],
        dimension_numbers=('NWC', 'WIO', 'NWC'), feature_group_count=C)
    return y + b

def lru_coeffs(xc, wa, ba, wx, bx, lam):
    B_, N, _ = xc.shape
    xh = xc.reshape(B_, N, LRU_HEADS, LRU_HD)
    r = jax.nn.sigmoid(jnp.einsum('bnhi,hij->bnhj', xh, wa).reshape(B_, N, W_LRU) + ba)
    i = jax.nn.sigmoid(jnp.einsum('bnhi,hij->bnhj', xh, wx).reshape(B_, N, W_LRU) + bx)
    log_a = (-LRU_C * r.astype(jnp.float32)) * jax.nn.softplus(-lam.astype(jnp.float32))
    a = jnp.exp(log_a)
    mult = jnp.sqrt(-jnp.expm1(2.0 * log_a))
    b = mult * (i * xc).astype(jnp.float32)
    return a, b

def _combine(left, right):
    a_l, b_l = left
    a_r, b_r = right
    return a_l * a_r, a_r * b_l + b_r

def linear_scan(a, b, h0, reverse):
    if h0 is not None:
        idx = -1 if reverse else 0
        b = b.at[:, idx].add(a[:, idx] * h0)
    _, h = lax.associative_scan(_combine, (a, b), reverse=reverse, axis=1)
    return h

def lru_branch(vx, vc, conv_w, conv_b, wa, ba, wx, bx, lam):
    pl = LRU_CONV // 2
    pr = LRU_CONV - 1 - pl
    xc = dwconv(vx, conv_w, conv_b, pl, pr)
    cc = dwconv(vc, conv_w, conv_b, pl, pr)
    y_x = jnp.zeros(vx.shape, jnp.float32)
    y_c = jnp.zeros(vc.shape, jnp.float32)
    for d, rev in enumerate((False, True)):
        a_c, b_c = lru_coeffs(cc, wa[d], ba[d], wx[d], bx[d], lam[d])
        h_c = linear_scan(a_c, b_c, None, rev)
        h0 = h_c[:, 0] if rev else h_c[:, -1]
        a_x, b_x = lru_coeffs(xc, wa[d], ba[d], wx[d], bx[d], lam[d])
        h_x = linear_scan(a_x, b_x, h0, rev)
        y_x = y_x + h_x
        y_c = y_c + h_c
    return y_x.astype(vx.dtype), y_c.astype(vc.dtype)

def pool_mixer(v, pool_w, pool_scale):
    B_, N, _ = v.shape
    v32 = v.astype(jnp.float32)
    cs = jnp.concatenate([jnp.zeros((B_, 1, W_POOL), jnp.float32), jnp.cumsum(v32, axis=1)], axis=1)
    t = jnp.arange(N)
    outs = []
    for gi, w in enumerate(POOL_WINDOWS):
        lo = jnp.clip(t - w // 2, 0, N)
        hi = jnp.clip(t + w // 2, 0, N)
        sl = cs[..., gi * POOL_GD:(gi + 1) * POOL_GD]
        mean = (jnp.take(sl, hi, axis=1) - jnp.take(sl, lo, axis=1)) / (hi - lo).astype(jnp.float32)[:, None]
        outs.append(mean - v32[..., gi * POOL_GD:(gi + 1) * POOL_GD])
    d = jnp.stack(outs, axis=2).astype(v.dtype)
    y = jnp.einsum('bngi,gij->bngj', d, pool_w).reshape(B_, N, W_POOL)
    return y * pool_scale

def conformer_conv(v, gg, dw, dw_b, ln_g, ln_b, pw):
    z = v * jax.nn.sigmoid(gg)
    z = dwconv(z, dw, dw_b, CONF_K // 2, CONF_K // 2)
    z32 = z.astype(jnp.float32)
    mu = jnp.mean(z32, axis=-1, keepdims=True)
    var = jnp.mean(jnp.square(z32 - mu), axis=-1, keepdims=True)
    z = ((z32 - mu) * lax.rsqrt(var + LN_EPS) * ln_g.astype(jnp.float32) + ln_b.astype(jnp.float32)).astype(v.dtype)
    z = jax.nn.silu(z)
    return jnp.einsum('bnc,ce->bne', z, pw)

def merge_out(y_lru, g_lru, y_pool, g_pool, y_conf, g_conf, w_out):
    z = jnp.concatenate([y_lru * jax.nn.silu(g_lru), y_pool * jax.nn.silu(g_pool),
                         y_conf * jax.nn.silu(g_conf)], axis=-1)
    return jnp.einsum('bnm,md->bnd', z, w_out)

def setup_inputs(seed: int = 0) -> dict:
    key = jax.random.key(seed)
    ks = jax.random.split(key, 24)
    f32 = jnp.float32
    def nrm(k, shape, s):
        return jax.random.normal(k, shape, f32) * s
    L = DEPTH
    x = nrm(ks[0], (BATCH, SEQ, D_MODEL), 1.0)
    c = nrm(ks[1], (BATCH, D_MODEL), 1.0)
    ctx = nrm(ks[2], (BATCH, CTX_LEN, D_MODEL), 1.0)
    c_ctx = nrm(ks[3], (D_MODEL,), 1.0)
    w_mod = nrm(ks[4], (L, D_MODEL, 3 * D_MODEL), 0.5 * D_MODEL ** -0.5)
    b_mod = nrm(ks[5], (L, 3 * D_MODEL), 0.02)
    g_pre = 1.0 + nrm(ks[6], (L, D_MODEL), 0.05)
    w_in = nrm(ks[7], (L, D_MODEL, N_IN), D_MODEL ** -0.5)
    lru_conv_w = nrm(ks[8], (L, LRU_CONV, W_LRU), LRU_CONV ** -0.5)
    lru_conv_b = nrm(ks[9], (L, W_LRU), 0.02)
    lru_wa = nrm(ks[10], (L, 2, LRU_HEADS, LRU_HD, LRU_HD), LRU_HD ** -0.5)
    lru_ba = nrm(ks[11], (L, 2, W_LRU), 0.02)
    lru_wx = nrm(ks[12], (L, 2, LRU_HEADS, LRU_HD, LRU_HD), LRU_HD ** -0.5)
    lru_bx = nrm(ks[13], (L, 2, W_LRU), 0.02)
    a_pow = jax.random.uniform(ks[14], (L, 2, W_LRU), f32, 0.9, 0.999)
    s = a_pow ** (1.0 / LRU_C)
    lru_lambda = jnp.log(s) - jnp.log1p(-s)
    pool_w = nrm(ks[15], (L, POOL_GROUPS, POOL_GD, POOL_GD), POOL_GD ** -0.5)
    pool_scale = 1.0 + nrm(ks[16], (L, W_POOL), 0.1)
    conf_dw = nrm(ks[17], (L, CONF_K, W_CONF), CONF_K ** -0.5)
    conf_dw_b = nrm(ks[18], (L, W_CONF), 0.02)
    conf_ln_g = 1.0 + nrm(ks[19], (L, W_CONF), 0.05)
    conf_ln_b = nrm(ks[20], (L, W_CONF), 0.02)
    conf_pw = nrm(ks[21], (L, W_CONF, W_CONF), W_CONF ** -0.5)
    w_out = nrm(ks[22], (L, W_MIX, D_MODEL), W_MIX ** -0.5)
    g_post = 1.0 + nrm(ks[23], (L, D_MODEL), 0.05)
    return {"x": x, "c": c, "ctx": ctx, "c_ctx": c_ctx, "w_mod": w_mod, "b_mod": b_mod,
            "g_pre": g_pre, "w_in": w_in, "lru_conv_w": lru_conv_w, "lru_conv_b": lru_conv_b,
            "lru_wa": lru_wa, "lru_ba": lru_ba, "lru_wx": lru_wx, "lru_bx": lru_bx,
            "lru_lambda": lru_lambda, "pool_w": pool_w, "pool_scale": pool_scale,
            "conf_dw": conf_dw, "conf_dw_b": conf_dw_b, "conf_ln_g": conf_ln_g, "conf_ln_b": conf_ln_b,
            "conf_pw": conf_pw, "w_out": w_out, "g_post": g_post}

def reference(x, c, ctx, c_ctx, w_mod, b_mod, g_pre, w_in, lru_conv_w, lru_conv_b, lru_wa, lru_ba,
              lru_wx, lru_bx, lru_lambda, pool_w, pool_scale, conf_dw, conf_dw_b, conf_ln_g, conf_ln_b,
              conf_pw, w_out, g_post):
    n = x.shape[1]
    x = x + pos_embed_2d(n).astype(x.dtype)[None]
    for l in range(DEPTH):
        need_ctx = l < DEPTH - 1
        sh_x, sc_x, gt_x = modulation(c, w_mod[l], b_mod[l])
        sh_c, sc_c, gt_c = modulation(c_ctx, w_mod[l], b_mod[l])
        hx = rmsnorm(x, g_pre[l]) * (1 + sc_x[:, None, :]) + sh_x[:, None, :]
        hc = rmsnorm(ctx, g_pre[l]) * (1 + sc_c) + sh_c
        ux = jnp.einsum('bnd,de->bne', hx, w_in[l])
        vx_lru, gx_lru, vx_pool, gx_pool, vx_conf, ggx_conf, gx_conf = jnp.split(ux, IN_SPLITS, axis=-1)
        if need_ctx:
            uc = jnp.einsum('bnd,de->bne', hc, w_in[l])
            vc_lru, gc_lru, vc_pool, gc_pool, vc_conf, ggc_conf, gc_conf = jnp.split(uc, IN_SPLITS, axis=-1)
        else:
            vc_lru = jnp.einsum('bnd,de->bne', hc, w_in[l][:, :W_LRU])

        y_lru_x, y_lru_c = lru_branch(vx_lru, vc_lru, lru_conv_w[l], lru_conv_b[l], lru_wa[l], lru_ba[l],
                                      lru_wx[l], lru_bx[l], lru_lambda[l])
        y_pool_x = pool_mixer(vx_pool, pool_w[l], pool_scale[l])
        y_conf_x = conformer_conv(vx_conf, ggx_conf, conf_dw[l], conf_dw_b[l], conf_ln_g[l], conf_ln_b[l], conf_pw[l])
        o_x = merge_out(y_lru_x, gx_lru, y_pool_x, gx_pool, y_conf_x, gx_conf, w_out[l])

        if need_ctx:
            y_pool_c = pool_mixer(vc_pool, pool_w[l], pool_scale[l])
            y_conf_c = conformer_conv(vc_conf, ggc_conf, conf_dw[l], conf_dw_b[l], conf_ln_g[l], conf_ln_b[l], conf_pw[l])
            o_c = merge_out(y_lru_c, gc_lru, y_pool_c, gc_pool, y_conf_c, gc_conf, w_out[l])
            ctx = ctx + gt_c * rmsnorm(o_c, g_post[l])

        x = x + gt_x[:, None, :] * rmsnorm(o_x, g_post[l])
    return x


_drawn_inputs = setup_inputs


def setup_inputs(seed=0):
    import zlib

    import numpy as np

    out = dict(_drawn_inputs(seed))
    spreads = {}
    factors = {'ctx': 35.646,
     'c_ctx': 3.617,
     'b_mod': 2.855,
     'g_pre': 3.268,
     'lru_conv_b': 15.57,
     'lru_wa': 2.756,
     'lru_ba': 200.0,
     'lru_bx': 37.963,
     'pool_scale': 8.0,
     'conf_dw': 3.083,
     'conf_dw_b': 48.609,
     'conf_ln_g': 24.066,
     'conf_ln_b': 57.371,
     'conf_pw': 2.944,
     'g_post': 5.179}
    for name, (base, spread) in spreads.items():
        noise = np.random.default_rng([zlib.crc32(name.encode()), seed]).standard_normal(out[name].shape)
        drawn = base * np.exp(spread * noise) if base else spread * noise
        out[name] = __import__('jax').numpy.asarray(drawn.astype(out[name].dtype))
    for name, factor in factors.items():
        out[name] = (out[name] * factor).astype(out[name].dtype)
    return out
```

```python
import concourse.bass as bass
from concourse import mybir
from contextlib import ExitStack

P = 128
D = 1024
SEQ = 2048
CTX = 256
KD = D // P
CH = 512
NCH = SEQ // CH
TPC = CH // P
NT_IN = 18
V_LRU, G_LRU, V_POOL, G_POOL, V_CONF, GG_CONF, G_CONF = 0, 4, 8, 10, 12, 14, 16
N_LRU = 4
CONF_K = 31
HALO = CONF_K // 2
PH = 8
EPS = 1e-6
LN_EPS = 1e-5

PAR = {}
_n = 0
for _name, _w in (("c", 16), ("b_mod", 16), ("g_pre", 8), ("lru_ba", 8), ("lru_bx", 8), ("lam", 8),
                  ("conv_w", 16), ("conv_b", 4), ("pool_scale", 2), ("conf_dw", 2 * CONF_K),
                  ("conf_dw_b", 2), ("ln_g", 2), ("ln_b", 2), ("pool_edge", 32)):
    PAR[_name] = _n
    _n += _w
N_PAR = _n

ORDER = [0, 1, 12, 14, 13, 15, 2, 3, 8, 9, 4, 5, 6, 7, 10, 11, 16, 17]
UNITS = [(o, c) for c in range(NCH) for o in (0, 1)] + [(o, c) for o in range(2, NT_IN) for c in range(NCH)]
N_CU = N_LRU


def unit_of(tile, chunk):
    return N_CU + UNITS.index((ORDER.index(tile), chunk))


STEPS = N_LRU * (NCH + 1)
PIECES = ["ctx", 0, NCH - 1, 1, 2]
NEW_PIECES = [[0], [1, 2], [3, 4], [], []]
GATES_AFTER = [8 + 5 * q // 2 for q in range(STEPS)]
CONF_FIRST = 4
CONF_JOBS = [(i, c) for c in range(NCH) for i in (0, 1)]


def splits_before(q):
    t, s = divmod(q, NCH + 1)
    return (2 * NCH + 1) * t + (2 * s - 1 if s else 0)


def mixer_kernel(nc, x, ctx, par, w_mod, b_gate, g_post, w_in, gate_w, pool_w, conf_pw, w_out,
                 pos_row, pos_col, u_dram, uc_dram, cv_dram, y_dram, out):
    f32 = mybir.dt.float32
    f32r = mybir.dt.float32r
    ACT = mybir.ActivationFunctionType
    ALU = mybir.AluOpType
    es = ExitStack()
    with es:
        base = (nc.sbuf_base + 31) // 32 * 32
        end = nc.sbuf_usable_end

        def at(name, shape, off, dt=f32):
            return nc.alloc_sbuf_tensor_at(name, shape, dt, offset=off)

        class Area:
            def __init__(self, off, limit):
                self.off, self.limit = off, limit

            def take(self, name, shape, dt=f32):
                t = at(name, shape, self.off, dt)
                n = 4
                for v in shape[1:]:
                    n *= v
                self.off += (n + 31) // 32 * 32
                assert self.off <= self.limit, (name, self.off, self.limit)
                return t

        fixed = Area(base, end)
        x0 = fixed.off
        xTh = fixed.take("xTh", [P, KD, SEQ], f32r)
        xTl = fixed.take("xTl", [P, KD, SEQ], f32r)
        w0 = fixed.off
        wh = fixed.take("wh", [P, 2, KD, P], f32r)
        wl = fixed.take("wl", [P, 2, KD, P], f32r)
        wraw = fixed.take("wraw", [P, KD, P])
        ustage = fixed.take("ustage", [P, 2, CH])
        prm = fixed.take("prm", [P, N_PAR])
        sml = fixed.take("sml", [P, 128])
        r0 = fixed.off
        wm = at("wm", [P, 8, KD, 256], x0)
        c3 = (NCH - 1) * CH
        a2 = Area(r0, end)
        xbuf = a2.take("xbuf", [P, 2, TPC, D])
        posr = a2.take("posr", [P, TPC, CH])
        posc = a2.take("posc", [P, CH])
        fbuf = a2.take("fbuf", [P, 4, CH])
        ident = a2.take("ident", [P, P])
        mrow = at("mrow", [2, 2 * D], x0 + 65536)
        a3 = Area(r0, end)
        xc = a3.take("xc", [P, CTX + SEQ])
        yrow = a3.take("yrow", [P, SEQ])
        vbuf = a3.take("vbuf", [P, 2, 3 + CH])
        sph = a3.take("sph", [P, 2, CH], f32r)
        spl = a3.take("spl", [P, 2, CH], f32r)
        Ib = a3.take("Ib", [P, 2, CH])
        Ab = a3.take("Ab", [P, 2, CH])
        Mb = a3.take("Mb", [P, 2, CH])
        Qb = a3.take("Qb", [P, 2, CH])
        gwh = a3.take("gwh", [P, 4, P], f32r)
        gwl = a3.take("gwl", [P, 4, P], f32r)
        gwr = a3.take("gwr", [P, 4, 64])
        cz = a3.take("cz", [P, CH + 2 * HALO])
        cg = a3.take("cg", [P, CH + 2 * HALO])
        a4 = Area(r0, end)
        la = a4.take("la", [P, 2, CH])
        lq = a4.take("lq", [P, 2, CH])
        lr = a4.take("lr", [P, 2, CH])
        lsh = a4.take("lsh", [P, 2, CH], f32r)
        lsl = a4.take("lsl", [P, 2, CH], f32r)
        ly = a4.take("ly", [P, 2, CH])
        lsd = a4.take("lsd", [P, CH])
        pyo = a4.take("pyo", [P, CH])
        pv = a4.take("pv", [P, CH + 2 * PH])
        pa = a4.take("pa", [P, CH + 2 * PH])
        pb = a4.take("pb", [P, CH + 2 * PH])
        pdh = a4.take("pdh", [P, CH], f32r)
        pdl = a4.take("pdl", [P, CH], f32r)
        py = a4.take("py", [P, CH])
        pwr = a4.take("pwr", [P, 2, P])
        pwh = a4.take("pwh", [P, 2, P], f32r)
        pwl = a4.take("pwl", [P, 2, P], f32r)
        cwr = a4.take("cwr", [P, 4, P])
        cwh = a4.take("cwh", [P, 4, P], f32r)
        cwl = a4.take("cwl", [P, 4, P], f32r)
        onesk = a4.take("onesk", [P, P])
        a5 = Area(x0, w0)
        woh = a5.take("woh", [P, KD, D], f32r)
        wol = a5.take("wol", [P, KD, D], f32r)
        z1 = a5.off
        zh = a5.take("zh", [P, 2, KD, CH], f32r)
        zl = a5.take("zl", [P, 2, KD, CH], f32r)
        wg = at("wg", [P, KD, D], z1 + 32768)
        wor = at("wor", [P, 4, D], w0)
        a6 = Area(r0, end)
        yb = a6.take("yb", [P, 3, CH])
        gb = a6.take("gb", [P, 3, CH])
        xres = a6.take("xres", [P, 2, D])
        tout = a6.take("tout", [P, 2, D])
        sqj = a6.take("sqj", [P, D])
        gbc = a6.take("gbc", [P, D])
        gpo = a6.take("gpo", [P, D])
        posr2 = a6.take("posr2", [P, 2, CH])
        posc2 = a6.take("posc2", [P, CH])
        crep = at("crep", [P, KD, P], w0 + 16384)

        def col(i, n=1):
            return sml[:, i:i + n]
        cs = col(0, 16)
        mo = 16
        kn, kp, k2 = col(48, 8), col(56, 8), col(64, 8)
        epsc, lnepsc = col(72), col(73)
        sq2 = col(74, 8)
        ssq = col(82, 4)
        rst = col(86, 8)
        carry = col(94, 2)
        lt = col(96, 32)
        ss2, ssum, rs2, rr2 = lt[:, 0:2], lt[:, 2:3], lt[:, 3:4], lt[:, 4:5]

        def par_col(name, i=0, n=1):
            return prm[:, PAR[name] + i:PAR[name] + i + n]

        bank = [es.enter_context(nc.psum_tensor(f"bank{i}", [P, CH], f32)) for i in range(8)]
        pu = bank[0:2]
        gp = bank[2:6]
        tp = bank[4:8]
        junk = bank[2:4]
        lmu, lvar, lpo, pmb = bank[2], bank[3], bank[4:6], bank[6:8]
        ob = [bank[0:2], bank[2:4], bank[4:6]]
        gob = bank[6:8]

        def sem(name):
            return es.enter_context(nc.semaphore(name))

        s_par, s_id, s_posc = sem("params_in"), sem("ident_ready"), sem("poscol_in")
        s_wm = [sem(f"wmod_in{m}") for m in range(8)]
        s_mrow, s_modT = sem("mod_rows"), sem("mod_turned")
        s_cs, s_mod, s_sc, s_kl = sem("silu_c"), sem("mod_psum"), sem("scales_ready"), sem("lru_consts")
        s_xin = [sem(f"x_in{b}") for b in range(2)]
        s_pr, s_pad, s_pcd = sem("posrow_in"), sem("posrow_added"), sem("poscol_added")
        s_sqh, s_ssum, s_el = sem("squares_half"), sem("square_sums"), sem("exp_lam")
        s_oss = sem("out_square_sum")
        s_sq, s_sd, s_xh = sem("squares"), sem("rms_root"), sem("xhat_ready")
        s_tp, s_f, s_hh, s_hl = sem("transposed"), sem("modulated"), sem("hT_hi"), sem("hT_lo")
        s_wr, s_whi, s_wlo = sem("w_raw_in"), sem("w_hi"), sem("w_lo")
        s_pu, s_ev = sem("unit_done"), sem("unit_evacuated")
        s_us = [sem(f"u_stored{b}") for b in range(2)]
        s_gz, s_gw, s_gwh, s_gwl = sem("gatew_zeroed"), sem("gatew_in"), sem("gatew_hi"), sem("gatew_lo")
        s_v, s_cv = [sem(f"v_in{b}") for b in range(2)], sem("convolved")
        s_sh, s_sl, s_pg, s_sig = sem("split_hi"), sem("split_lo"), sem("gates_done"), sem("sigmoids")
        s_aq, s_exp, s_m2, s_rt = sem("a_and_q"), sem("tanhs"), sem("one_minus_a2"), sem("roots")
        s_ix, s_st, s_ya, s_ys = sem("gated_input"), sem("scan_done"), sem("y_added"), sem("y_stored")
        s_cl, s_cgs, s_ct, s_cst = sem("conf_in"), sem("conf_sigmoid"), sem("conf_taps"), sem("conf_stored")
        s_dve = sem("dve_chain")
        s_pool = sem("pool_chain")
        s_tw, s_twz, s_twh, s_twl = sem("tailw_in"), sem("tailw_zero"), sem("tailw_hi"), sem("tailw_lo")
        s_la, s_mu, s_zc, s_lsq, s_var = sem("ln_in"), sem("ln_mean"), sem("ln_centred"), sem("ln_squares"), sem("ln_var")
        s_lsd, s_lzn, s_lsi, s_lhi, s_llo = sem("ln_root"), sem("ln_normed"), sem("ln_silu"), sem("ln_hi"), sem("ln_lo")
        s_lpw, s_lye, s_lys = sem("conf_product"), sem("conf_y"), sem("conf_y_stored")
        s_pvi, s_psm, s_pd, s_pdh, s_pdl = sem("pool_in"), sem("pool_sums"), sem("pool_diff"), sem("pool_hi"), sem("pool_lo")
        s_pmm, s_pye, s_pys = sem("pool_product"), sem("pool_y"), sem("pool_y_stored")
        s_wor, s_woh, s_wol = [sem(f"wo_in{b}") for b in range(4)], sem("wo_hi"), sem("wo_lo")
        s_wg, s_cr, s_gmm, s_gbc, s_gpo = sem("wgate_in"), sem("c_repeated"), sem("gate_product"), sem("gate_row"), sem("gpost_in")
        s_yg = [sem(f"yg_in{b}") for b in range(3)]
        s_sg, s_z, s_zh, s_zl = sem("gate_silu"), sem("z_ready"), sem("z_hi"), sem("z_lo")
        s_om, s_osq, s_ort, s_ot = sem("out_product"), sem("out_squares"), sem("out_root"), sem("out_scaled")
        s_xr = [sem(f"xres_in{b}") for b in range(2)]
        s_xp, s_of = sem("xres_pos"), sem("out_final")
        s_out = [sem(f"out_stored{b}") for b in range(2)]
        s_p2c = sem("poscol2_in")

        block = es.enter_context(nc.Block())

        GROUPS = [("ctx", CTX // P)] + [(c, TPC) for c in range(NCH)]

        def tiles_before(g):
            return 0 if g == 0 else CTX // P + TPC * (g - 1)

        def group_cols(g):
            return (c3, c3 + CTX) if g == 0 else ((g - 1) * CH, g * CH)

        def w_tiles(hi, o):
            return [hi[:, o, k, :] for k in range(KD)]

        def w_place(hi, lo, o):
            return hi[:, o % 2], lo[:, o % 2]

        def early_w(t):
            if t < 2:
                return wh[:, t], wl[:, t]
            a = c3 + CTX + (t - 2) * P
            return xTh[:, :, a:a + P], xTl[:, :, a:a + P]

        W_JOBS = [(t, early_w(t)) for t in range(4)] + [(ORDER[o], (wh[:, o % 2], wl[:, o % 2])) for o in range(2, NT_IN)]

        def w_slot_free(w):
            if w < 4:
                return 0
            o = w - 2 - 2
            return N_CU + max(n for n, (oo, c) in enumerate(UNITS) if oo == o) + 1

        def w_job_of(o):
            return o if o < 2 else o + 2

        def step_chunks(s):
            return (None, None) if s == 0 else (s - 1, NCH - s)

        def xc_piece(c):
            return xc[:, 0:CTX] if c is None or c == "ctx" else xc[:, CTX + c * CH:CTX + (c + 1) * CH]

        LN_JOBS = list(range(NCH))
        POOL_JOBS = [(i, c) for c in range(NCH) for i in (0, 1)]
        TAIL = []
        rest = list(range(GATES_AFTER[-1] + 1, len(UNITS)))

        def some_unit():
            if rest:
                TAIL.append(("unit", rest.pop(0)))

        for c in range(NCH):
            for token in (("mu", c), ("pool", 2 * c), None, ("var", c), None, ("pmm", 2 * c), ("pool", 2 * c + 1),
                          None, ("pw", c), None, ("pmm", 2 * c + 1)):
                TAIL.append(token) if token else some_unit()
        while rest:
            some_unit()
        ITEMS = [(c, k) for c in range(NCH) for k in range(KD)]
        TILES = [(c, i) for c in range(NCH) for i in range(TPC)]
        STAGE5 = [("item", n) for n in range(KD)]
        for n, (c, i) in enumerate(TILES):
            STAGE5.append(("tile", n))
            if c + 1 < NCH:
                STAGE5 += [("item", (c + 1) * KD + m) for m in range(3 * i, min(3 * i + 3, KD))]

        @block.sync
        def _(sp):
            sp.dma_start(prm[:], par).then_inc(s_par, 16)

            def load_group(g):
                if g >= 2:
                    sp.wait_ge(s_tp, 8 * (g - 1))
                src = ctx if g == 0 else x[(g - 1) * CH:g * CH, :]
                n = GROUPS[g][1]
                sp.dma_start(xbuf[:, g % 2, 0:n, :], src.rearrange("(i p) d -> p i d", p=P)).then_inc(s_xin[g % 2], 16)
                if g >= 1:
                    if g >= 2:
                        sp.wait_ge(s_pad, TPC * (g - 1))
                    sp.dma_start(posr[:], pos_row[g - 1]).then_inc(s_pr, 16)

            def load_w(w):
                if w >= 1:
                    sp.wait_ge(s_wlo, w)
                sp.dma_start(wraw[:], w_in[W_JOBS[w][0]]).then_inc(s_wr, 16)

            def store_out(n):
                sp.wait_ge(s_of, n + 1)
                sp.dma_start(out[n * P:(n + 1) * P, :], tout[:, n % 2, :]).then_inc(s_out[n % 2], 16)

            for m in range(8):
                sp.dma_start(wm[:, m], w_mod[m]).then_inc(s_wm[m], 16)
                if m == 0:
                    load_w(0)
                if m == 3:
                    load_group(0)
                if m == 6:
                    load_w(1)
            sp.dma_start(posc[:], pos_col).then_inc(s_posc, 16)
            load_group(1)

            def store_u(U):
                sp.wait_ge(s_ev, U + 1)
                if U < N_CU:
                    dst, n = uc_dram[U], CTX
                else:
                    o, c = UNITS[U - N_CU]
                    dst, n = u_dram[ORDER[o], :, c * CH:(c + 1) * CH], CH
                sp.dma_start(dst, ustage[:, U % 2, 0:n]).then_inc(s_us[U % 2], 16)

            load_w(2)
            load_w(3)
            load_group(2)
            for U in range(N_CU):
                store_u(U)
            for n in range(GATES_AFTER[-1] + 1):
                if n in (0, 2):
                    load_group(3 + n // 2)
                if n == 3:
                    load_w(4)
                store_u(N_CU + n)
                if n % 4 == 2 and n >= 6:
                    load_w((n + 2) // 4 + 3)
            for kind, n in TAIL:
                if kind == "unit":
                    store_u(N_CU + n)
                    if n % 4 == 2 and (n + 2) // 4 + 3 < len(W_JOBS):
                        load_w((n + 2) // 4 + 3)
                if kind == "pmm":
                    i, c = POOL_JOBS[n]
                    sp.wait_ge(s_pye, n + 1)
                    sp.dma_start(y_dram[4 + i, :, c * CH:(c + 1) * CH], pyo[:]).then_inc(s_pys, 16)
                if kind == "pw":
                    sp.wait_ge(s_lye, 2 * n + 2)
                    for i in range(2):
                        sp.dma_start(y_dram[6 + i, :, n * CH:(n + 1) * CH], ly[:, i, :]).then_inc(s_lys, 16)

            sp.wait_ge(s_pu, N_CU + len(UNITS))
            for m in range(4):
                sp.dma_start(wg[:, :, m * 256:(m + 1) * 256], w_mod[8 + m]).then_inc(s_wg, 16)
            for k in range(KD):
                if k >= 4:
                    sp.wait_ge(s_wol, k - 3)
                sp.dma_start(wor[:, k % 4, :], w_out[k * P:(k + 1) * P, :]).then_inc(s_wor[k % 4], 16)
            sp.wait_ge(s_lys, 32 * NCH)
            sp.wait_ge(s_pys, 32 * NCH)
            sp.dma_start(gbc[:], b_gate.partition_broadcast(P)).then_inc(s_gpo, 16)
            sp.dma_start(gpo[:], g_post.partition_broadcast(P)).then_inc(s_gpo, 16)
            sp.dma_start(posc2[:], pos_col).then_inc(s_p2c, 16)
            for kind, n in STAGE5:
                if kind == "item":
                    c, k = ITEMS[n]
                    if n >= 3:
                        sp.wait_ge(s_zl, n - 2)
                    sp.dma_start(yb[:, n % 3, :], y_dram[k, :, c * CH:(c + 1) * CH]).then_inc(s_yg[n % 3], 16)
                    gt = (G_LRU + k) if k < 4 else (G_POOL + k - 4) if k < 6 else (G_CONF + k - 6)
                    sp.dma_start(gb[:, n % 3, :], u_dram[gt, :, c * CH:(c + 1) * CH]).then_inc(s_yg[n % 3], 16)
                else:
                    if n >= 2:
                        sp.wait_ge(s_of, n - 1)
                    sp.dma_start(xres[:, n % 2, :], x[n * P:(n + 1) * P, :]).then_inc(s_xr[n % 2], 16)
                    sp.dma_start(posr2[:, n % 2, :], pos_row[n // TPC, :, n % TPC, :]).then_inc(s_xr[n % 2], 16)
                    if n >= 1:
                        store_out(n - 1)
            store_out(len(TILES) - 1)
            for b in range(2):
                sp.wait_ge(s_out[b], 16 * len(TILES) // 2)

        @block.gpsimd
        def _(pool):
            g = nc.gpsimd

            def round_hi(dst, src):
                return g.tensor_scalar(dst, src, 1.0, 1.0, ALU.mult, ALU.mult)

            g.memset(ident[:], 0.0).then_inc(s_id, 1)
            pool.wait_ge(s_id, 1)
            g.affine_select(out=ident[:], in_=ident[:], compare_op=ALU.not_equal, fill=1.0, base=0,
                            pattern=[[-1, P]], channel_multiplier=1).then_inc(s_id, 1)

            def add_rows(gi):
                for i in range(TPC):
                    if i == 0:
                        pool.wait_ge(s_xin[gi % 2], 16 * (gi // 2 + 1))
                        pool.wait_ge(s_pr, 16 * gi)
                    g.tensor_tensor(out=xbuf[:, gi % 2, i, 0:CH], in0=xbuf[:, gi % 2, i, 0:CH],
                                    in1=posr[:, i, :], op=ALU.add).then_inc(s_pad, 1)

            def hi_group(gi):
                a, b = group_cols(gi)
                for k in range(KD):
                    idx = 8 * gi + k
                    pool.wait_ge(s_f, idx + 1)
                    if gi == NCH and k == 0:
                        pool.wait_ge(s_pu, N_CU)
                    round_hi(xTh[:, k, a:b], fbuf[:, idx % 4, 0:b - a]).then_inc(s_hh, 1)

            for gi in range(NCH + 1):
                if gi < NCH:
                    add_rows(gi + 1)
                hi_group(gi)
            pool.wait_ge(s_hl, 8 * (NCH + 1))
            g.memset(gwh[:].bitcast(f32), 0.0).then_inc(s_gz, 1)
            g.memset(gwl[:].bitcast(f32), 0.0).then_inc(s_gz, 1)

            def load_gate_w(t):
                if t:
                    pool.wait_ge(s_gwl, 2 * t)
                g.dma_start(gwr[:], gate_w[t]).then_inc(s_gw, 16)

            def load_v(p):
                t, j = divmod(p, NCH + 1)
                if p >= 2:
                    pool.wait_ge(s_cv, p - 1)
                c = PIECES[j]
                if c == "ctx":
                    pool.wait_ge(s_us[t % 2], 16 * (t // 2 + 1))
                    g.dma_start(vbuf[:, p % 2, 2:2 + CTX], uc_dram[t]).then_inc(s_v[p % 2], 16)
                else:
                    a, b = max(c * CH - 2, 0), min((c + 1) * CH + 1, SEQ)
                    U = unit_of(V_LRU + t, NCH - 1)
                    for back in (0, 1):
                        pool.wait_ge(s_us[(U - back) % 2], 16 * ((U - back) // 2 + 1))
                    off = a - (c * CH - 2)
                    g.dma_start(vbuf[:, p % 2, off:off + b - a], u_dram[V_LRU + t, :, a:b]).then_inc(s_v[p % 2], 16)

            def gate_w_hi(t):
                pool.wait_ge(s_gw, 16 * (t + 1))
                if t:
                    pool.wait_ge(s_pg, (NCH + 1) * t)
                else:
                    pool.wait_ge(s_gz, 2)
                for i, h in enumerate((slice(0, 64), slice(64, 128))):
                    round_hi(gwh[h, :, h], gwr[h]).then_inc(s_gwh, 1)
                    pool.wait_ge(s_gwh, 2 * t + i + 1)

            def split_hi(q):
                t, s = divmod(q, NCH + 1)
                pool.wait_ge(s_cv, (NCH + 1) * t + max((p for ss in range(s + 1) for p in NEW_PIECES[ss]), default=0) + 1)
                if q:
                    pool.wait_ge(s_pg, q)
                f, b = step_chunks(s)
                if s == 0:
                    round_hi(sph[:, 0, 0:CTX], xc_piece(None)).then_inc(s_sh, 1)
                else:
                    round_hi(sph[:, 0, :], xc_piece(f)).then_inc(s_sh, 1)
                    round_hi(sph[:, 1, :], xc_piece(b)).then_inc(s_sh, 1)

            def gated_input(q):
                s = q % (NCH + 1)
                f, b = step_chunks(s)
                n = CTX if s == 0 else CH
                for d, c in enumerate((f, b)):
                    pool.wait_ge(s_sig, 4 * q + 2 * d + 2)
                    g.tensor_tensor(out=Ib[:, d, 0:n], in0=Ib[:, d, 0:n], in1=xc_piece(c), op=ALU.mult).then_inc(s_ix, 1)

            def add_y(q):
                t, s = divmod(q, NCH + 1)
                if s < 3:
                    return
                for d, c in enumerate(step_chunks(s)):
                    pool.wait_ge(s_st, 2 * q + d + 1)
                    yc = yrow[:, c * CH:(c + 1) * CH]
                    g.tensor_tensor(out=yc, in0=yc, in1=Qb[:, d, :], op=ALU.add).then_inc(s_ya, 1)
                pool.wait_ge(s_ya, 4 * t + 2 * (s - 3) + 2)
                for c in step_chunks(s):
                    g.dma_start(y_dram[t, :, c * CH:(c + 1) * CH], yrow[:, c * CH:(c + 1) * CH]).then_inc(s_ys, 16)

            def load_conf(j):
                i, c = CONF_JOBS[j]
                if j:
                    pool.wait_ge(s_cst, 16 * j)
                for tile in (V_CONF + i, GG_CONF + i):
                    U = unit_of(tile, min(c + 1, NCH - 1))
                    for back in (0, 1):
                        pool.wait_ge(s_us[(U - back) % 2], 16 * ((U - back) // 2 + 1))
                a, b = max(c * CH - HALO, 0), min((c + 1) * CH + HALO, SEQ)
                off = a - (c * CH - HALO)
                g.dma_start(cz[:, off:off + b - a], u_dram[V_CONF + i, :, a:b]).then_inc(s_cl, 16)
                g.dma_start(cg[:, off:off + b - a], u_dram[GG_CONF + i, :, a:b]).then_inc(s_cl, 16)

            def store_conf(j):
                i, c = CONF_JOBS[j]
                pool.wait_ge(s_ct, j + 1)
                g.dma_start(cv_dram[i, :, c * CH:(c + 1) * CH], cg[:, 0:CH]).then_inc(s_cst, 16)

            load_gate_w(0)
            load_v(0)
            load_v(1)
            gate_w_hi(0)
            split_hi(0)
            load_v(2)
            for q in range(STEPS):
                t, s = divmod(q, NCH + 1)
                if s == NCH and t + 1 < N_LRU:
                    gate_w_hi(t + 1)
                if q + 1 < STEPS:
                    split_hi(q + 1)
                if s == 0:
                    load_v((NCH + 1) * t + 3)
                    load_v((NCH + 1) * t + 4)
                if s == 2 and t + 1 < N_LRU:
                    load_gate_w(t + 1)
                    load_v((NCH + 1) * (t + 1))
                    load_v((NCH + 1) * (t + 1) + 1)
                if s == NCH and t + 1 < N_LRU:
                    load_v((NCH + 1) * (t + 1) + 2)
                gated_input(q)
                j, half = divmod(q - CONF_FIRST + 1, 2)
                if half == 0 and 0 <= j < len(CONF_JOBS):
                    if j:
                        store_conf(j - 1)
                    load_conf(j)
                add_y(q)
            store_conf(len(CONF_JOBS) - 1)

            pool.wait_ge(s_ys, 64 * N_LRU)
            pool.wait_ge(s_cst, 16 * len(CONF_JOBS))
            g.memset(pwr[:], 0.0).then_inc(s_twz, 1)
            g.memset(onesk[:], 1.0 / 256.0).then_inc(s_twz, 1)
            pool.wait_ge(s_twz, 1)
            for h in range(2):
                g.dma_start(pwr[64 * h:64 * h + 64, :, 64 * h:64 * h + 64], pool_w[h]).then_inc(s_tw, 16)
            g.dma_start(cwr[:], conf_pw).then_inc(s_tw, 16)
            pool.wait_ge(s_tw, 48)
            round_hi(pwh[:], pwr[:]).then_inc(s_twh, 1)
            round_hi(cwh[:], cwr[:]).then_inc(s_twh, 1)

            def load_pool(n):
                i, c = POOL_JOBS[n]
                if n:
                    pool.wait_ge(s_pd, n)
                U = unit_of(V_POOL + i, NCH - 1)
                for back in (0, 1):
                    pool.wait_ge(s_us[(U - back) % 2], 16 * ((U - back) // 2 + 1))
                a, b = max(c * CH - PH, 0), min((c + 1) * CH + PH, SEQ)
                off = a - (c * CH - PH)
                if c == 0:
                    g.memset(pv[:, 0:PH], 0.0).then_inc(s_pool, 1)
                if c == NCH - 1:
                    g.memset(pv[:, PH + CH:], 0.0).then_inc(s_pool, 1)
                g.dma_start(pv[:, off:off + b - a], u_dram[V_POOL + i, :, a:b]).then_inc(s_pvi, 16)

            def load_ln(n):
                if n:
                    pool.wait_ge(s_zc, 2 * n)
                g.dma_start(la[:], cv_dram[:, :, n * CH:(n + 1) * CH].rearrange("i p n -> p i n")).then_inc(s_la, 16)

            W2 = CH + 2 * PH
            chain = [0]

            def link(ins):
                chain[0] += 1
                ins.then_inc(s_pool, 1)
                pool.wait_ge(s_pool, chain[0])

            def pool_sums(n):
                i, c = POOL_JOBS[n]
                chain[0] += (c == 0) + (c == NCH - 1)
                if chain[0]:
                    pool.wait_ge(s_pool, chain[0])
                pool.wait_ge(s_pvi, 16 * (n + 1))
                h = slice(64, 128)
                add = ALU.add
                link(g.tensor_tensor(out=pa[:, 0:W2 - 1], in0=pv[:, 0:W2 - 1], in1=pv[:, 1:W2], op=add))
                if i == 0:
                    g.tensor_tensor(out=pb[h, 0:W2 - 3], in0=pa[h, 0:W2 - 3], in1=pa[h, 2:W2 - 1], op=add).then_inc(s_psm, 1)
                else:
                    link(g.tensor_tensor(out=pb[:, 0:W2 - 3], in0=pa[:, 0:W2 - 3], in1=pa[:, 2:W2 - 1], op=add))
                    link(g.tensor_tensor(out=pa[:, 0:W2 - 7], in0=pb[:, 0:W2 - 7], in1=pb[:, 4:W2 - 3], op=add))
                    g.tensor_tensor(out=pb[h, 0:W2 - 15], in0=pa[h, 0:W2 - 15], in1=pa[h, 8:W2 - 7], op=add).then_inc(s_psm, 1)

            def pool_hi(n):
                pool.wait_ge(s_pd, n + 1)
                if n:
                    pool.wait_ge(s_pmm, n)
                round_hi(pdh[:], py[:]).then_inc(s_pdh, 1)

            def ln_hi(n):
                for m in range(2):
                    pool.wait_ge(s_lsi, 2 * n + m + 1)
                    if n and m == 0:
                        pool.wait_ge(s_lpw, 2 * n)
                    round_hi(lsh[:, m, :], lq[:, m, :]).then_inc(s_lhi, 1)

            load_pool(0)
            load_ln(0)
            for kind, n in TAIL:
                if kind == "pool":
                    pool_sums(n)
                    pool_hi(n)
                    if n + 1 < len(POOL_JOBS):
                        load_pool(n + 1)
                if kind == "var":
                    ln_hi(n)
                    if n + 1 < NCH:
                        load_ln(n + 1)

            for kind, n in STAGE5:
                if kind == "item":
                    c, k = ITEMS[n]
                    pool.wait_ge(s_z, n + 1)
                    if c >= 2 and k == 0:
                        pool.wait_ge(s_om, TPC * (c - 1))
                    round_hi(zh[:, c % 2, k, :], yb[:, n % 3, :]).then_inc(s_zh, 1)
                else:
                    pool.wait_ge(s_xr[n % 2], 32 * (n // 2 + 1))
                    if n == 0:
                        pool.wait_ge(s_p2c, 16)
                    g.tensor_tensor(out=xres[:, n % 2, 0:CH], in0=xres[:, n % 2, 0:CH], in1=posr2[:, n % 2, :],
                                    op=ALU.add).then_inc(s_xp, 1)
                    g.tensor_tensor(out=xres[:, n % 2, CH:D], in0=xres[:, n % 2, CH:D], in1=posc2[:],
                                    op=ALU.add).then_inc(s_xp, 1)

        @block.scalar
        def _(act):
            a = nc.scalar
            act.wait_ge(s_par, 16)
            a.activation(cs, par_col("c", 0, 16), ACT.Silu).then_inc(s_cs, 1)
            a.activation(lt[:, 0:8], par_col("lam", 0, 8), ACT.Abs).then_inc(s_el, 1)
            act.wait_ge(s_el, 1)
            a.activation(lt[:, 8:16], lt[:, 0:8], ACT.Exp, scale=-1.0).then_inc(s_el, 1)

            def w_hi(w):
                act.wait_ge(s_wr, 16 * (w + 1))
                if w_slot_free(w):
                    act.wait_ge(s_pu, w_slot_free(w))
                if w in (2, 3):
                    act.wait_ge(s_mod, 8)
                a.activation(W_JOBS[w][1][0], wraw[:], ACT.Copy).then_inc(s_whi, 1)

            def squares(gi):
                for i in range(GROUPS[gi][1]):
                    T = tiles_before(gi) + i
                    if gi == 0:
                        if i == 0:
                            act.wait_ge(s_xin[0], 16)
                    else:
                        act.wait_ge(s_pad, TPC * (gi - 1) + i + 1)
                        act.wait_ge(s_pcd, TPC * (gi - 1) + i + 1)
                    if T:
                        act.wait_ge(s_sq, T)
                        act.wait_ge(s_sqh, T)
                    if i == 0 and gi:
                        act.wait_ge(s_xh, gi)
                    a.activation(junk[0][:], xbuf[:, gi % 2, i, 0:CH], ACT.Square,
                                 accum_out=sq2[:, 2 * i:2 * i + 1]).then_inc(s_sqh, 1)
                    a.activation(junk[1][:], xbuf[:, gi % 2, i, CH:D], ACT.Square,
                                 accum_out=sq2[:, 2 * i + 1:2 * i + 2]).then_inc(s_sq, 1)

            def root(gi):
                act.wait_ge(s_ssum, gi + 1)
                n = GROUPS[gi][1]
                a.activation(rst[:, 0:n], ssq[:, 0:n], ACT.Sqrt, bias=epsc, scale=1.0 / D).then_inc(s_sd, 1)

            def modulate(gi, ks=range(KD)):
                n = GROUPS[gi][1] * P
                so = mo + (16 if gi == 0 else 0)
                for k in ks:
                    idx = 8 * gi + k
                    act.wait_ge(s_tp, idx + 1)
                    if idx >= 4:
                        act.wait_ge(s_hh, idx - 3)
                        act.wait_ge(s_hl, idx - 3)
                    a.activation(fbuf[:, idx % 4, 0:n], tp[idx % 4][:, 0:n], ACT.Identity,
                                 scale=col(so + k), bias=col(so + 8 + k)).then_inc(s_f, 1)

            def evac(U):
                act.wait_ge(s_pu, U + 1)
                if U >= 2:
                    act.wait_ge(s_us[U % 2], 16 * (U // 2))
                n = CTX if U < N_CU else CH
                a.activation(ustage[:, U % 2, 0:n], pu[U % 2][:, 0:n], ACT.Copy).then_inc(s_ev, 1)

            def sigmoids(q):
                t, s = divmod(q, NCH + 1)
                n = CTX if s == 0 else CH
                act.wait_ge(s_pg, q + 1)
                for d in range(2):
                    if q:
                        act.wait_ge(s_st, 2 * (q - 1) + d + 1)
                    a.activation(Mb[:, d, 0:n], gp[2 * d][:, 0:n], ACT.Sigmoid,
                                 bias=par_col("lru_ba", 4 * d + t)).then_inc(s_sig, 1)
                    a.activation(Ib[:, d, 0:n], gp[2 * d + 1][:, 0:n], ACT.Sigmoid,
                                 bias=par_col("lru_bx", 4 * d + t)).then_inc(s_sig, 1)

            def decays(q):
                t, s = divmod(q, NCH + 1)
                n = CTX if s == 0 else CH
                for d in range(2):
                    kc = 4 * d + t
                    act.wait_ge(s_sig, 4 * q + 2 * d + 1)
                    if s == 0 and t or s == 4:
                        act.wait_ge(s_ya, 4 * t if s == 0 else 4 * t + 2)
                    a.activation(Ab[:, d, 0:n], Mb[:, d, 0:n], ACT.Exp, scale=kn[:, kc:kc + 1]).then_inc(s_aq, 1)
                    a.activation(Qb[:, d, 0:n], Mb[:, d, 0:n], ACT.Exp, scale=k2[:, kc:kc + 1]).then_inc(s_aq, 1)
                    a.activation(Mb[:, d, 0:n], Mb[:, d, 0:n], ACT.Tanh, scale=kp[:, kc:kc + 1]).then_inc(s_exp, 1)

            def roots(q):
                s = q % (NCH + 1)
                n = CTX if s == 0 else CH
                for d in range(2):
                    act.wait_ge(s_m2, 2 * q + d + 1)
                    a.activation(Mb[:, d, 0:n], Mb[:, d, 0:n], ACT.Sqrt).then_inc(s_rt, 1)

            def conf_sigmoid(j):
                i, c = CONF_JOBS[j]
                lo = HALO if c == 0 else 0
                hi = CH + HALO if c == NCH - 1 else CH + 2 * HALO
                act.wait_ge(s_cl, 32 * (j + 1))
                a.activation(cg[:, lo:hi], cg[:, lo:hi], ACT.Sigmoid).then_inc(s_cgs, 1)

            w_hi(0)
            w_hi(1)
            squares(0)
            root(0)
            squares(1)
            act.wait_ge(s_sc, 1)
            modulate(0)
            w_hi(2)
            w_hi(3)
            root(1)
            for U in range(N_CU):
                evac(U)
            squares(2)
            modulate(1)
            root(2)
            for gi in range(1, NCH + 1):
                if gi < NCH:
                    modulate(gi + 1, range(0, 4))
                if gi + 2 <= NCH:
                    squares(gi + 2)
                evac(N_CU + 2 * gi - 2)
                if gi < NCH:
                    modulate(gi + 1, range(4, KD))
                if gi + 2 <= NCH:
                    root(gi + 2)
                if gi == NCH:
                    w_hi(4)
                evac(N_CU + 2 * gi - 1)

            def unit_side(n):
                if n % 4 == 0 and n // 4 + 3 < len(W_JOBS):
                    w_hi(n // 4 + 3)
                evac(N_CU + n)

            n = 8
            for q in range(STEPS):
                sigmoids(q)
                j, half = divmod(q - CONF_FIRST, 2)
                if half == 0 and 0 <= j < len(CONF_JOBS):
                    conf_sigmoid(j)
                upto = GATES_AFTER[q + 1] if q + 1 < STEPS else GATES_AFTER[-1] + 1
                first = n
                while n < min(first + 1, upto):
                    unit_side(n)
                    n += 1
                decays(q)
                while n < min(first + 2, upto):
                    unit_side(n)
                    n += 1
                roots(q)
                while n < upto:
                    unit_side(n)
                    n += 1

            def pool_evac(m):
                i, c = POOL_JOBS[m]
                act.wait_ge(s_pmm, m + 1)
                if m:
                    act.wait_ge(s_pys, 16 * m)
                a.activation(pyo[:], pmb[m % 2][:], ACT.Copy, scale=par_col("pool_scale", i)).then_inc(s_pye, 1)

            def ln_squares(m):
                for i in range(2):
                    act.wait_ge(s_zc, 2 * m + i + 1)
                    if m and i == 0:
                        act.wait_ge(s_llo, 2 * m)
                    a.activation(lq[:, i, :], lr[:, i, :], ACT.Square).then_inc(s_lsq, 1)

            def ln_root_swish(m):
                act.wait_ge(s_var, m + 1)
                if m:
                    act.wait_ge(s_lzn, 2 * m)
                a.activation(lsd[:], lvar[:], ACT.Sqrt, bias=lnepsc).then_inc(s_lsd, 1)
                for i in range(2):
                    act.wait_ge(s_lzn, 2 * m + i + 1)
                    a.activation(lq[:, i, :], lr[:, i, :], ACT.Silu, scale=par_col("ln_g", i),
                                 bias=par_col("ln_b", i)).then_inc(s_lsi, 1)

            def conf_evac(m):
                for i in range(2):
                    act.wait_ge(s_lpw, 2 * m + i + 1)
                    if m and i == 0:
                        act.wait_ge(s_lys, 32 * m)
                    a.activation(ly[:, i, :], lpo[i][:], ACT.Copy).then_inc(s_lye, 1)

            for kind, m in TAIL:
                if kind == "unit":
                    unit_side(m)
                if kind == "mu":
                    ln_squares(m)
                if kind == "var":
                    ln_root_swish(m)
                if kind == "pmm":
                    pool_evac(m)
                if kind == "pw":
                    conf_evac(m)

            def out_weights_hi(k):
                act.wait_ge(s_wor[k % 4], 16 * (k // 4 + 1))
                if k == 0:
                    act.wait_ge(s_pu, N_CU + len(UNITS))
                a.activation(woh[:, k, :], wor[:, k % 4, :], ACT.Copy).then_inc(s_woh, 1)

            for k in range(KD):
                out_weights_hi(k)
            for kind, m in STAGE5:
                if kind == "item":
                    act.wait_ge(s_yg[m % 3], 32 * (m // 3 + 1))
                    a.activation(gb[:, m % 3, :], gb[:, m % 3, :], ACT.Silu).then_inc(s_sg, 1)
                else:
                    act.wait_ge(s_om, m + 1)
                    if m:
                        act.wait_ge(s_oss, m)
                        act.wait_ge(s_osq, 2 * m)
                    for h in range(2):
                        a.activation(sqj[:, h * CH:(h + 1) * CH], ob[m % 3][h][:], ACT.Square,
                                     accum_out=ss2[:, h:h + 1]).then_inc(s_osq, 1)
                    act.wait_ge(s_oss, m + 1)
                    if m:
                        act.wait_ge(s_ot, m)
                    a.activation(rs2, ssum, ACT.Sqrt, bias=epsc, scale=1.0 / D).then_inc(s_ort, 1)

        @block.vector
        def _(dve):
            v = nc.vector
            chain = [0]

            def link(ins):
                chain[0] += 1
                ins.then_inc(s_dve, 1)
                dve.wait_ge(s_dve, chain[0])

            def stt(out, in0, sc, in1, op0, op1):
                return v.scalar_tensor_tensor(out=out, in0=in0, scalar=sc, in1=in1, op0=op0, op1=op1)

            v.memset(epsc, EPS).then_inc(s_kl, 1)
            v.memset(lnepsc, LN_EPS).then_inc(s_kl, 1)
            dve.wait_ge(s_el, 2)
            e, y, y2, sr = lt[:, 8:16], lt[:, 0:8], lt[:, 16:24], lt[:, 24:32]
            link(v.tensor_scalar(y2, e, 2.0, None, ALU.add))
            link(v.reciprocal(y2, y2))
            link(v.tensor_tensor(out=y, in0=e, in1=y2, op=ALU.mult))
            link(v.tensor_tensor(out=y2, in0=y, in1=y, op=ALU.mult))
            link(v.tensor_scalar(sr, y2, 1.0 / 21.0, 1.0 / 19.0, ALU.mult, ALU.add))
            for j in range(17, 0, -2):
                link(v.tensor_tensor(out=sr, in0=sr, in1=y2, op=ALU.mult))
                link(v.tensor_scalar(sr, sr, 1.0 / j, None, ALU.add))
            link(v.tensor_tensor(out=sr, in0=sr, in1=y, op=ALU.mult))
            link(v.tensor_scalar(y, par_col("lam", 0, 8), -1.0, 0.0, ALU.mult, ALU.max))
            link(stt(sr, sr, 2.0, y, ALU.mult, ALU.add))
            link(v.tensor_scalar(kp, sr, 8.0, None, ALU.mult))
            link(v.tensor_scalar(k2, sr, -16.0, None, ALU.mult))
            v.tensor_scalar(kn, sr, -8.0, None, ALU.mult).then_inc(s_kl, 1)

            def w_lo(w):
                dve.wait_ge(s_whi, w + 1)
                h, l = W_JOBS[w][1]
                v.tensor_tensor(out=l, in0=wraw[:], in1=h.bitcast(f32), op=ALU.subtract).then_inc(s_wlo, 1)

            def add_cols(gi):
                for i in range(TPC):
                    if i == 0:
                        dve.wait_ge(s_xin[gi % 2], 16 * (gi // 2 + 1))
                        dve.wait_ge(s_posc, 16)
                    v.tensor_tensor(out=xbuf[:, gi % 2, i, CH:D], in0=xbuf[:, gi % 2, i, CH:D], in1=posc[:],
                                    op=ALU.add).then_inc(s_pcd, 1)

            def normalise(gi):
                n = GROUPS[gi][1]
                dve.wait_ge(s_sq, tiles_before(gi) + n)
                v.tensor_tensor(out=ssq[:, 0:n], in0=sq2[:, 0:2 * n:2], in1=sq2[:, 1:2 * n:2], op=ALU.add).then_inc(s_ssum, 1)
                dve.wait_ge(s_sd, gi + 1)
                link(v.reciprocal(rst[:, 4:4 + n], rst[:, 0:n]))
                for i in range(n):
                    ins = v.tensor_scalar(xbuf[:, gi % 2, i, :], xbuf[:, gi % 2, i, :], rst[:, 4 + i:5 + i], None, ALU.mult)
                ins.then_inc(s_xh, 1)

            def lo_group(gi):
                a, b = group_cols(gi)
                for k in range(KD):
                    idx = 8 * gi + k
                    dve.wait_ge(s_hh, idx + 1)
                    v.tensor_tensor(out=xTl[:, k, a:b], in0=fbuf[:, idx % 4, 0:b - a],
                                    in1=xTh[:, k, a:b].bitcast(f32), op=ALU.subtract).then_inc(s_hl, 1)

            def mod_rows():
                for m in range(4):
                    dve.wait_ge(s_mod, 2 * m + 2)
                    v.tensor_copy(mrow[:, m * CH:(m + 1) * CH], bank[4 + m][0:2, :]).then_inc(s_mrow, 1)

            def scales():
                dve.wait_ge(s_modT, 4)
                m = bank[0][:, 0:32].rearrange("p (m s) -> p s m", s=2)
                for s, off in ((0, mo), (1, mo + 16)):
                    link(stt(col(off, 8), m[:, s, 8:16], 1.0, par_col("b_mod", 8, 8), ALU.add, ALU.add))
                    link(v.tensor_tensor(out=col(off, 8), in0=col(off, 8), in1=par_col("g_pre", 0, 8), op=ALU.mult))
                    link(v.tensor_tensor(out=col(off + 8, 8), in0=m[:, s, 0:8], in1=par_col("b_mod", 0, 8), op=ALU.add))
                v.memset(carry, 0.0).then_inc(s_sc, 1)

            w_lo(0)
            w_lo(1)
            add_cols(1)
            normalise(0)
            mod_rows()
            scales()
            lo_group(0)
            w_lo(2)
            w_lo(3)
            normalise(1)
            add_cols(2)
            for gi in range(1, NCH + 1):
                lo_group(gi)
                if gi < NCH:
                    normalise(gi + 1)
                if gi + 2 <= NCH:
                    add_cols(gi + 2)
            w_lo(4)

            def gate_w_lo(t):
                for i, h in enumerate((slice(0, 64), slice(64, 128))):
                    dve.wait_ge(s_gwh, 2 * t + i + 1)
                    v.tensor_tensor(out=gwl[h, :, h], in0=gwr[h], in1=gwh[h, :, h].bitcast(f32),
                                    op=ALU.subtract).then_inc(s_gwl, 1)

            def conv(p):
                t, j = divmod(p, NCH + 1)
                c = PIECES[j]
                n = CTX if c == "ctx" else CH
                dst = xc_piece(c)
                vb = vbuf[:, p % 2, :]
                if c in ("ctx", 0):
                    link(v.memset(vb[:, 0:2], 0.0))
                if c in ("ctx", NCH - 1):
                    link(v.memset(vb[:, 2 + n:3 + n], 0.0))
                dve.wait_ge(s_v[p % 2], 16 * (p // 2 + 1))
                if t and j == 0:
                    dve.wait_ge(s_ix, 2 * (NCH + 1) * (t - 1) + 2)
                elif t:
                    dve.wait_ge(s_ix, 2 * (NCH + 1) * t)
                w = [par_col("conv_w", 4 * t + i) for i in range(4)]
                link(v.tensor_scalar(dst, vb[:, 0:n], w[0], par_col("conv_b", t), ALU.mult, ALU.add))
                link(stt(dst, vb[:, 1:1 + n], w[1], dst, ALU.mult, ALU.add))
                link(stt(dst, vb[:, 2:2 + n], w[2], dst, ALU.mult, ALU.add))
                stt(dst, vb[:, 3:3 + n], w[3], dst, ALU.mult, ALU.add).then_inc(s_cv, 1)
                dve.wait_ge(s_cv, p + 1)

            def split_lo(q):
                s = q % (NCH + 1)
                f, b = step_chunks(s)
                for d, c in enumerate((f,) if s == 0 else (f, b)):
                    n = CTX if s == 0 else CH
                    dve.wait_ge(s_sh, splits_before(q) + d + 1)
                    v.tensor_tensor(out=spl[:, d, 0:n], in0=xc_piece(c), in1=sph[:, d, 0:n].bitcast(f32),
                                    op=ALU.subtract).then_inc(s_sl, 1)

            def one_minus_a2(q):
                n = CTX if q % (NCH + 1) == 0 else CH
                for d in range(2):
                    dve.wait_ge(s_exp, 2 * q + d + 1)
                    stt(Mb[:, d, 0:n], Qb[:, d, 0:n], 1.0, Mb[:, d, 0:n], ALU.add, ALU.mult).then_inc(s_m2, 1)

            def scans(q):
                t, s = divmod(q, NCH + 1)
                n = CTX if s == 0 else CH
                for d, c in enumerate(step_chunks(s)):
                    dve.wait_ge(s_rt, 2 * q + d + 1)
                    dve.wait_ge(s_ix, 2 * q + d + 1)
                    link(v.tensor_tensor(out=Ib[:, d, 0:n], in0=Ib[:, d, 0:n], in1=Mb[:, d, 0:n], op=ALU.mult))
                    if s in (1, 2):
                        if t:
                            dve.wait_ge(s_ys, 64 * t)
                        o = yrow[:, c * CH:(c + 1) * CH]
                    else:
                        o = Qb[:, d, 0:n]
                    A, B, O = Ab[:, d, 0:n], Ib[:, d, 0:n], o
                    if d:
                        A, B, O = A[:, ::-1], B[:, ::-1], o[:, ::-1]
                    ins = v.tensor_tensor_scan(out=O, data0=A, data1=B, initial=0.0 if s == 0 else carry[:, d:d + 1],
                                               op0=ALU.mult, op1=ALU.add)
                    if s == NCH:
                        ins.then_inc(s_st, 1)
                    else:
                        link(ins)
                        last = o[:, 0:1] if d else o[:, n - 1:n]
                        v.tensor_copy(carry[:, d:d + 1], last).then_inc(s_st, 1)
                        dve.wait_ge(s_st, 2 * q + d + 1)

            def glu(j):
                i, c = CONF_JOBS[j]
                lo = HALO if c == 0 else 0
                hi = CH + HALO if c == NCH - 1 else CH + 2 * HALO
                dve.wait_ge(s_cgs, j + 1)
                link(v.tensor_tensor(out=cz[:, lo:hi], in0=cz[:, lo:hi], in1=cg[:, lo:hi], op=ALU.mult))
                if c == 0:
                    link(v.memset(cz[:, 0:HALO], 0.0))
                if c == NCH - 1:
                    link(v.memset(cz[:, CH + HALO:], 0.0))

            def taps(j, k0, k1):
                i, c = CONF_JOBS[j]
                acc = cg[:, 0:CH]
                for k in range(k0, k1):
                    w = par_col("conf_dw", CONF_K * i + k)
                    if k == 0:
                        link(v.tensor_scalar(acc, cz[:, 0:CH], w, par_col("conf_dw_b", i), ALU.mult, ALU.add))
                    elif k < CONF_K - 1:
                        link(stt(acc, cz[:, k:k + CH], w, acc, ALU.mult, ALU.add))
                    else:
                        stt(acc, cz[:, k:k + CH], w, acc, ALU.mult, ALU.add).then_inc(s_ct, 1)

            conv(0)
            gate_w_lo(0)
            split_lo(0)
            conv(1)
            conv(2)
            done_w = 5
            for q in range(STEPS):
                t, s = divmod(q, NCH + 1)
                if s == NCH and t + 1 < N_LRU:
                    conv((NCH + 1) * (t + 1))
                    gate_w_lo(t + 1)
                if q + 1 < STEPS:
                    split_lo(q + 1)
                if s == 0:
                    conv((NCH + 1) * t + 3)
                    conv((NCH + 1) * t + 4)
                j, half = divmod(q - CONF_FIRST, 2)
                on = 0 <= j < len(CONF_JOBS)
                if on and half == 0:
                    glu(j)
                    taps(j, 0, 12)
                if on and half == 1:
                    taps(j, 16, CONF_K)
                one_minus_a2(q)
                if on and half == 0:
                    taps(j, 12, 16)
                scans(q)
                upto = GATES_AFTER[q + 1] if q + 1 < STEPS else GATES_AFTER[-1] + 1
                while done_w < len(W_JOBS) and 4 * (done_w - 3) < upto:
                    w_lo(done_w)
                    done_w += 1
                if s == NCH and t + 1 < N_LRU:
                    conv((NCH + 1) * (t + 1) + 1)
                    conv((NCH + 1) * (t + 1) + 2)

            dve.wait_ge(s_twh, 2)
            v.tensor_tensor(out=pwl[:], in0=pwr[:], in1=pwh[:].bitcast(f32), op=ALU.subtract).then_inc(s_twl, 1)
            v.tensor_tensor(out=cwl[:], in0=cwr[:], in1=cwh[:].bitcast(f32), op=ALU.subtract).then_inc(s_twl, 1)

            def pool_diff(n):
                i, c = POOL_JOBS[n]
                dve.wait_ge(s_psm, n + 1)
                if n:
                    dve.wait_ge(s_pdh, n)
                    dve.wait_ge(s_pdl, n)
                w_lo_, w_hi_ = (2, 4) if i == 0 else (8, 16)
                for h, w, src in ((slice(0, 64), w_lo_, pa), (slice(64, 128), w_hi_, pb)):
                    o = PH - w // 2
                    if c == 0:
                        link(v.tensor_tensor(out=src[h, o:o + 8], in0=src[h, o:o + 8],
                                             in1=prm[h, PAR["pool_edge"] + 16 * i:PAR["pool_edge"] + 16 * i + 8], op=ALU.mult))
                    if c == NCH - 1:
                        link(v.tensor_tensor(out=src[h, o + CH - 8:o + CH], in0=src[h, o + CH - 8:o + CH],
                                             in1=prm[h, PAR["pool_edge"] + 16 * i + 8:PAR["pool_edge"] + 16 * i + 16], op=ALU.mult))
                    ins = stt(py[h, :], src[h, o:o + CH], 1.0 / w, pv[h, PH:PH + CH], ALU.mult, ALU.subtract)
                ins.then_inc(s_pd, 1)
                dve.wait_ge(s_pdh, n + 1)
                v.tensor_tensor(out=pdl[:], in0=py[:], in1=pdh[:].bitcast(f32), op=ALU.subtract).then_inc(s_pdl, 1)

            def ln_centre(n):
                dve.wait_ge(s_mu, n + 1)
                if n:
                    dve.wait_ge(s_lsi, 2 * n)
                for i in range(2):
                    v.tensor_tensor(out=lr[:, i, :], in0=la[:, i, :], in1=lmu[:], op=ALU.subtract).then_inc(s_zc, 1)

            def ln_norm(n):
                dve.wait_ge(s_lsd, n + 1)
                link(v.reciprocal(lsd[:], lsd[:]))
                for i in range(2):
                    v.tensor_tensor(out=lr[:, i, :], in0=lr[:, i, :], in1=lsd[:], op=ALU.mult).then_inc(s_lzn, 1)
                for i in range(2):
                    dve.wait_ge(s_lhi, 2 * n + i + 1)
                    v.tensor_tensor(out=lsl[:, i, :], in0=lq[:, i, :], in1=lsh[:, i, :].bitcast(f32),
                                    op=ALU.subtract).then_inc(s_llo, 1)

            for kind, n in TAIL:
                if kind == "pool":
                    pool_diff(n)
                if kind == "mu":
                    ln_centre(n)
                if kind == "var":
                    ln_norm(n)
                if kind == "unit" and n % 4 == 0 and done_w < len(W_JOBS):
                    w_lo(done_w)
                    done_w += 1

            dve.wait_ge(s_wlo, len(W_JOBS))
            v.tensor_copy(crep[:], cs[:, 0:16:2].unsqueeze(2).to_broadcast([P, KD, P])).then_inc(s_cr, 1)
            for k in range(KD):
                dve.wait_ge(s_woh, k + 1)
                v.tensor_tensor(out=wol[:, k, :], in0=wor[:, k % 4, :], in1=woh[:, k, :].bitcast(f32),
                                op=ALU.subtract).then_inc(s_wol, 1)
            dve.wait_ge(s_gpo, 32)
            dve.wait_ge(s_gmm, 2)
            for h in range(2):
                hs = slice(h * CH, (h + 1) * CH)
                link(v.tensor_tensor(out=gbc[:, hs], in0=gbc[:, hs], in1=gob[h][:], op=ALU.add))
                link(v.tensor_tensor(out=gbc[:, hs], in0=gbc[:, hs], in1=gpo[:, hs], op=ALU.mult))
            for kind, n in STAGE5:
                if kind == "item":
                    c, k = ITEMS[n]
                    dve.wait_ge(s_sg, n + 1)
                    v.tensor_tensor(out=yb[:, n % 3, :], in0=yb[:, n % 3, :], in1=gb[:, n % 3, :], op=ALU.mult).then_inc(s_z, 1)
                    dve.wait_ge(s_zh, n + 1)
                    v.tensor_tensor(out=zl[:, c % 2, k, :], in0=yb[:, n % 3, :], in1=zh[:, c % 2, k, :].bitcast(f32),
                                    op=ALU.subtract).then_inc(s_zl, 1)
                else:
                    dve.wait_ge(s_osq, 2 * n + 2)
                    v.tensor_tensor(out=ssum, in0=ss2[:, 0:1], in1=ss2[:, 1:2], op=ALU.add).then_inc(s_oss, 1)
                    dve.wait_ge(s_ort, n + 1)
                    link(v.reciprocal(rr2, rs2))
                    if n >= 2:
                        dve.wait_ge(s_out[n % 2], 16 * (n // 2))
                    for h in range(2):
                        hs = slice(h * CH, (h + 1) * CH)
                        ins = stt(tout[:, n % 2, hs], ob[n % 3][h][:], rr2, gbc[:, hs], ALU.mult, ALU.mult)
                    ins.then_inc(s_ot, 1)
                    dve.wait_ge(s_ot, n + 1)
                    dve.wait_ge(s_xp, 2 * n + 2)
                    v.tensor_tensor(out=tout[:, n % 2, :], in0=tout[:, n % 2, :], in1=xres[:, n % 2, :],
                                    op=ALU.add).then_inc(s_of, 1)

        @block.tensor
        def _(pe):
            mm = nc.tensor.matmul

            def mm3(out, wh_, wl_, xh_, xl_, first, last):
                mm(out, wh_, xh_, start=first, stop=False)
                mm(out, wh_, xl_, start=False, stop=False)
                return mm(out, wl_, xh_, start=False, stop=last)

            pe.wait_ge(s_cs, 1)
            for m in range(8):
                pe.wait_ge(s_wm[m], 16)
                for k in range(KD):
                    ins = mm(bank[4 + m // 2][0:2, (m % 2) * 256:(m % 2) * 256 + 256], cs[:, 2 * k:2 * k + 2],
                             wm[:, m, k, :], start=(k == 0), stop=(k == KD - 1))
                ins.then_inc(s_mod, 1)
            pe.wait_ge(s_id, 2)
            for m in range(4):
                pe.wait_ge(s_mrow, m + 1)
                for j in range(4):
                    mt = 4 * m + j
                    ins = nc.tensor.transpose(bank[0][:, 2 * mt:2 * mt + 2], mrow[:, mt * P:(mt + 1) * P], ident[0:2, 0:2])
                ins.then_inc(s_modT, 1)

            def transposes(gi, ks=range(KD)):
                pe.wait_ge(s_xh, gi + 1)
                if gi == 0:
                    pe.wait_ge(s_id, 2)
                for k in ks:
                    idx = 8 * gi + k
                    if idx >= 4:
                        pe.wait_ge(s_f, idx - 3)
                    for i in range(GROUPS[gi][1]):
                        ins = nc.tensor.transpose(tp[idx % 4][:, i * P:(i + 1) * P],
                                                  xbuf[:, gi % 2, i, k * P:(k + 1) * P], ident[:])
                    ins.then_inc(s_tp, 1)

            def project(U, h, l, a, b):
                if U >= 2:
                    pe.wait_ge(s_ev, U - 1)
                for k in range(KD):
                    ins = mm3(pu[U % 2][:, 0:b - a], h[:, k, :], l[:, k, :], xTh[:, k, a:b], xTl[:, k, a:b],
                              k == 0, k == KD - 1)
                ins.then_inc(s_pu, 1)

            def unit(n):
                o, c = UNITS[n]
                w = w_job_of(o)
                pe.wait_ge(s_wlo, w + 1)
                pe.wait_ge(s_hl, 8 * (c + 2))
                project(N_CU + n, wh[:, o % 2], wl[:, o % 2], c * CH, (c + 1) * CH)

            def gates(q):
                t, s = divmod(q, NCH + 1)
                n = CTX if s == 0 else CH
                if s == 0:
                    pe.wait_ge(s_gwl, 2 * t + 2)
                pe.wait_ge(s_sl, splits_before(q + 1))
                if q:
                    pe.wait_ge(s_sig, 4 * q)
                for m in range(4):
                    d = 0 if s == 0 else m // 2
                    ins = mm3(gp[m][:, 0:n], gwh[:, m, :], gwl[:, m, :], sph[:, d, 0:n], spl[:, d, 0:n], True, True)
                ins.then_inc(s_pg, 1)

            transposes(0)
            pe.wait_ge(s_sc, 1)
            pe.wait_ge(s_hl, 8)
            for U in range(N_CU):
                pe.wait_ge(s_wlo, U + 1)
                h, l = early_w(U)
                project(U, h, l, c3, c3 + CTX)
            transposes(1)
            for gi in range(1, NCH + 1):
                if gi < NCH:
                    transposes(gi + 1, range(0, 4))
                unit(2 * gi - 2)
                if gi < NCH:
                    transposes(gi + 1, range(4, KD))
                unit(2 * gi - 1)
            q = 0
            for n in range(8, GATES_AFTER[-1] + 1):
                unit(n)
                if q < STEPS and GATES_AFTER[q] == n:
                    gates(q)
                    q += 1
            assert q == STEPS
            pe.wait_ge(s_twl, 2)
            pe.wait_ge(s_twz, 2)
            for kind, n in TAIL:
                if kind == "unit":
                    unit(n)
                if kind == "mu":
                    pe.wait_ge(s_la, 16 * (n + 1))
                    if n:
                        pe.wait_ge(s_zc, 2 * n)
                    else:
                        pe.wait_ge(s_sig, 4 * STEPS)
                    for i in range(2):
                        ins = mm(lmu[:], onesk[:], la[:, i, :], start=(i == 0), stop=(i == 1))
                    ins.then_inc(s_mu, 1)
                if kind == "var":
                    pe.wait_ge(s_lsq, 2 * n + 2)
                    if n:
                        pe.wait_ge(s_lsd, n)
                    for i in range(2):
                        ins = mm(lvar[:], onesk[:], lq[:, i, :], start=(i == 0), stop=(i == 1))
                    ins.then_inc(s_var, 1)
                if kind == "pw":
                    pe.wait_ge(s_llo, 2 * n + 2)
                    if n:
                        pe.wait_ge(s_lye, 2 * n)
                    for m in range(2):
                        for k in range(2):
                            ins = mm3(lpo[m][:], cwh[:, 2 * k + m, :], cwl[:, 2 * k + m, :], lsh[:, k, :], lsl[:, k, :],
                                      k == 0, k == 1)
                        ins.then_inc(s_lpw, 1)
                if kind == "pmm":
                    i, c = POOL_JOBS[n]
                    pe.wait_ge(s_pdl, n + 1)
                    if n >= 2:
                        pe.wait_ge(s_pye, n - 1)
                    mm3(pmb[n % 2][:], pwh[:, i, :], pwl[:, i, :], pdh[:], pdl[:], True, True).then_inc(s_pmm, 1)

            pe.wait_ge(s_cr, 1)
            pe.wait_ge(s_wg, 64)
            pe.wait_ge(s_pye, 2 * NCH)
            for h in range(2):
                for k in range(KD):
                    ins = mm(gob[h][:], crep[:, k, :], wg[:, k, h * CH:(h + 1) * CH], start=(k == 0), stop=(k == KD - 1))
                ins.then_inc(s_gmm, 1)
            pe.wait_ge(s_wol, KD)
            pe.wait_ge(s_ev, N_CU + len(UNITS))
            pe.wait_ge(s_lye, 2 * NCH)
            for n, (c, i) in enumerate(TILES):
                pe.wait_ge(s_zl, KD * (c + 1))
                if n >= 3:
                    pe.wait_ge(s_ot, n - 2)
                for h in range(2):
                    hs = slice(h * CH, (h + 1) * CH)
                    for k in range(KD):
                        zs = slice(i * P, (i + 1) * P)
                        ins = mm3(ob[n % 3][h][:], zh[:, c % 2, k, zs], zl[:, c % 2, k, zs], woh[:, k, hs], wol[:, k, hs],
                                  k == 0, k == KD - 1)
                ins.then_inc(s_om, 1)


def position_tables():
    import numpy as np
    q = D // 4
    omega = (np.float32(1.0) / (np.float32(10000.0) ** (np.arange(q, dtype=np.float32) / np.float32(q)))).astype(np.float32)

    def enc(p):
        ang = p.astype(np.float32)[:, None] * omega[None, :]
        return np.concatenate([np.sin(ang), np.cos(ang)], axis=-1).astype(np.float32)
    row = enc(np.arange(SEQ) // 64).reshape(NCH, TPC, P, D // 2).transpose(0, 2, 1, 3)
    return np.ascontiguousarray(row), enc(np.arange(P) % 64)


def pool_edges():
    import numpy as np
    e = np.ones((P, 2, 2, PH), np.float32)
    for i, h, w in ((0, 0, 2), (0, 1, 4), (1, 0, 8), (1, 1, 16)):
        for t in range(PH):
            e[64 * h:64 * h + 64, i, 0, t] = w / min(w, t + w // 2)
            back = PH - t
            e[64 * h:64 * h + 64, i, 1, t] = w / min(w, back + w // 2)
    return e.reshape(P, 32)


def kernel(**inputs):
    import numpy as np
    import concourse.bacc as bacc
    from concourse import mybir as mb
    from concourse.bass_utils import run_bass_kernel_spmd

    a = {k: np.asarray(v) for k, v in inputs.items()}

    def cols(v):
        return v.reshape(-1, P).T

    c2 = np.stack([a["c"][0].reshape(KD, P), a["c_ctx"].reshape(KD, P)], axis=1).reshape(2 * KD, P).T
    par = np.concatenate([
        c2, cols(a["b_mod"][0, :2 * D]), cols(a["g_pre"][0]), cols(a["lru_ba"][0]), cols(a["lru_bx"][0]),
        cols(a["lru_lambda"][0]), cols(a["lru_conv_w"][0].reshape(4, N_LRU, P).transpose(1, 0, 2)),
        cols(a["lru_conv_b"][0]), cols(a["pool_scale"][0]),
        cols(a["conf_dw"][0].reshape(CONF_K, 2, P).transpose(1, 0, 2)), cols(a["conf_dw_b"][0]),
        cols(a["conf_ln_g"][0]), cols(a["conf_ln_b"][0]), pool_edges()], axis=1)
    gw = np.stack([a["lru_wa"][0], a["lru_wx"][0]], axis=1)
    gw = gw.reshape(2, 2, N_LRU, 2, 64, 64).transpose(2, 3, 4, 0, 1, 5).reshape(N_LRU, P, 4, 64)
    pw = a["pool_w"][0].reshape(2, 2, 64, 64).transpose(1, 2, 0, 3)
    cw = a["conf_pw"][0].reshape(2, P, 2, P).transpose(1, 0, 2, 3).reshape(P, 4, P)
    pos_row, pos_col = position_tables()
    arrays = {
        "x": a["x"][0], "ctx": a["ctx"][0], "par": par,
        "w_mod": a["w_mod"][0].reshape(KD, P, 12, 256).transpose(2, 1, 0, 3),
        "b_gate": a["b_mod"][0, 2 * D:], "g_post": a["g_post"][0],
        "w_in": a["w_in"][0].reshape(KD, P, NT_IN, P).transpose(2, 1, 0, 3),
        "gate_w": gw, "pool_w": pw, "conf_pw": cw, "w_out": a["w_out"][0],
        "pos_row": pos_row, "pos_col": pos_col,
    }
    nc = bacc.Bacc("TRN2", target_bir_lowering=False, num_devices=1)
    f32 = mb.dt.float32
    feed, args = {}, []
    for name, v in arrays.items():
        v = np.ascontiguousarray(v)
        feed[f"in_{name}"] = v
        args.append(nc.dram_tensor(f"in_{name}", v.shape, mb.dt.from_np(v.dtype), kind="ExternalInput").ap())
    for name, shape in (("u", (NT_IN, P, SEQ)), ("uc", (N_LRU, P, CTX)), ("cv", (2, P, SEQ)), ("y", (KD, P, SEQ))):
        args.append(nc.dram_tensor(f"scratch_{name}", shape, f32, kind="Internal").ap())
    args.append(nc.dram_tensor("out_0", (SEQ, D), f32, kind="ExternalOutput").ap())
    mixer_kernel(nc, *args)
    r = run_bass_kernel_spmd(nc, [feed], core_ids=[0])
    return r.results[0]["out_0"].reshape(1, SEQ, D)
```

```python
import concourse.bass as bass
from concourse import mybir
from contextlib import ExitStack

P = 128
D = 1024
SEQ = 2048
CTX = 256
KD = D // P
CH = 512
NCH = SEQ // CH
TPC = CH // P
NT_IN = 18
V_LRU, G_LRU, V_POOL, G_POOL, V_CONF, GG_CONF, G_CONF = 0, 4, 8, 10, 12, 14, 16
N_LRU = 4
CONF_K = 31
HALO = CONF_K // 2
PH = 8
EPS = 1e-6
LN_EPS = 1e-5

PAR = {}
_n = 0
for _name, _w in (("c", 16), ("b_mod", 16), ("g_pre", 8), ("lru_ba", 8), ("lru_bx", 8), ("lam", 8),
                  ("conv_w", 16), ("conv_b", 4), ("pool_scale", 2), ("conf_dw", 2 * CONF_K),
                  ("conf_dw_b", 2), ("ln_g", 2), ("ln_b", 2), ("pool_edge", 32)):
    PAR[_name] = _n
    _n += _w
N_PAR = _n

ORDER = [0, 1, 12, 14, 13, 15, 2, 3, 8, 9, 4, 5, 6, 7, 10, 11, 16, 17]
UNITS = [(o, c) for c in range(NCH) for o in (0, 1)] + [(o, c) for o in range(2, NT_IN) for c in range(NCH)]
N_CU = N_LRU


def unit_of(tile, chunk):
    return N_CU + UNITS.index((ORDER.index(tile), chunk))


STEPS = N_LRU * (NCH + 1)
PIECES = ["ctx", 1, 0, NCH - 1, 2]
LAST_PIECE = [0, 3, 4, 4, 4]
LAST_USE = [0, 3, NCH, NCH, 3]
CONF_FIRST = 3
GATES_AFTER = [8 + 2 * min(q, CONF_FIRST) + 27 * max(q - CONF_FIRST, 0) // 10 for q in range(STEPS)]
CONF_JOBS = [(i, c) for i in (0, 1) for c in range(NCH)]
TAPS_IN_STEP = [13, 14, 18, 16, 13]


def tap_plan():
    taps = [(j, k) for j in range(len(CONF_JOBS)) for k in range(CONF_K)]
    plan = [[] for _ in range(STEPS)]
    for q in range(CONF_FIRST, STEPS):
        n = TAPS_IN_STEP[q % (NCH + 1)] if q + 1 < STEPS else len(taps)
        plan[q], taps = taps[:n], taps[n:]
    first = [min(q for q in range(STEPS) if (j, 0) in plan[q]) for j in range(len(CONF_JOBS))]
    last = [max(q for q in range(STEPS) if (j, CONF_K - 1) in plan[q]) for j in range(len(CONF_JOBS))]
    return plan, first, last


TAPS_BEHIND = 5
SIDE_BEHIND = ("mu", "pmm", "pw", "pool")
SIDE_PIECES = 2
TAP_PLAN, JOB_FIRST, JOB_LAST = tap_plan()
JOB_LOAD = [CONF_FIRST - 1, CONF_FIRST] + [JOB_LAST[j - 2] + 1 for j in range(2, len(CONF_JOBS))]
assert all(l < f for l, f in zip(JOB_LOAD, JOB_FIRST))


def splits_before(q):
    t, s = divmod(q, NCH + 1)
    return (2 * NCH + 1) * t + (2 * s - 1 if s else 0)


def mixer_kernel(nc, x, ctx, par, w_mod, b_gate, g_post, w_in, gate_w, pool_w, conf_pw, w_out,
                 pos_row, pos_col, u_dram, uc_dram, cv_dram, y_dram, out):
    f32 = mybir.dt.float32
    f32r = mybir.dt.float32r
    ACT = mybir.ActivationFunctionType
    ALU = mybir.AluOpType
    es = ExitStack()
    with es:
        base = (nc.sbuf_base + 31) // 32 * 32
        end = nc.sbuf_usable_end

        def at(name, shape, off, dt=f32):
            return nc.alloc_sbuf_tensor_at(name, shape, dt, offset=off)

        class Area:
            def __init__(self, off, limit):
                self.off, self.limit = off, limit

            def take(self, name, shape, dt=f32):
                t = at(name, shape, self.off, dt)
                n = 4
                for v in shape[1:]:
                    n *= v
                self.off += (n + 31) // 32 * 32
                assert self.off <= self.limit, (name, self.off, self.limit)
                return t

        fixed = Area(base, end)
        x0 = fixed.off
        xTh = fixed.take("xTh", [P, KD, SEQ], f32r)
        xTl = fixed.take("xTl", [P, KD, SEQ], f32r)
        w0 = fixed.off
        wh = fixed.take("wh", [P, 2, KD, P], f32r)
        wl = fixed.take("wl", [P, 2, KD, P], f32r)
        wraw = fixed.take("wraw", [P, KD, P])
        ustage = fixed.take("ustage", [P, 2, CH])
        prm = fixed.take("prm", [P, N_PAR])
        sml = fixed.take("sml", [P, 128])
        r0 = fixed.off
        wm = at("wm", [P, 8, KD, 256], x0)
        xg = at("xg", [P, KD, SEQ], x0 + 4 * KD * SEQ)
        c3 = (NCH - 1) * CH
        a2 = Area(r0, end)
        cbuf = a2.take("cbuf", [P, CTX // P, KD, P])
        hcl = a2.take("hcl", [P, KD, CTX], f32r)
        ewl = a2.take("ewl", [P, 2, KD, P], f32r)
        posr = a2.take("posr", [P, TPC, CH])
        posc = a2.take("posc", [P, CH])
        fbuf = a2.take("fbuf", [P, 4, CH])
        ident = a2.take("ident", [P, P])
        mrow = a2.take("mrow", [2, 2 * D])
        a3 = Area(r0, end)
        xc = a3.take("xc", [P, CTX + SEQ])
        yrow = a3.take("yrow", [P, SEQ])
        vbuf = a3.take("vbuf", [P, 2, 3 + CH])
        sph = a3.take("sph", [P, 2, CH], f32r)
        spl = a3.take("spl", [P, 2, CH], f32r)
        Ib = a3.take("Ib", [P, 2, CH])
        Ab = a3.take("Ab", [P, 2, CH])
        Qb = a3.take("Qb", [P, 2, CH])
        gwh = a3.take("gwh", [P, 4, P], f32r)
        gwl = a3.take("gwl", [P, 4, P], f32r)
        gwr = a3.take("gwr", [P, 4, 64])
        czb = a3.take("czb", [P, 2, CH + 2 * HALO])
        cgb = a3.take("cgb", [P, 2, CH + 2 * HALO])
        a4 = Area(r0, end)
        la = a4.take("la", [P, 2, CH])
        lq = a4.take("lq", [P, 2, CH])
        lr = a4.take("lr", [P, 2, 2, CH])
        lsh = a4.take("lsh", [P, 2, CH], f32r)
        lsl = a4.take("lsl", [P, 2, CH], f32r)
        ly = a4.take("ly", [P, 2, CH])
        lsd = a4.take("lsd", [P, CH])
        pyo = a4.take("pyo", [P, CH])
        pv = a4.take("pv", [P, CH + 2 * PH])
        pa = a4.take("pa", [P, CH + 2 * PH])
        pb = a4.take("pb", [P, CH + 2 * PH])
        pdh = a4.take("pdh", [P, CH], f32r)
        pdl = a4.take("pdl", [P, CH], f32r)
        py = a4.take("py", [P, CH])
        pwr = a4.take("pwr", [P, 2, P])
        pwh = a4.take("pwh", [P, 2, P], f32r)
        pwl = a4.take("pwl", [P, 2, P], f32r)
        cwr = a4.take("cwr", [P, 4, P])
        cwh = a4.take("cwh", [P, 4, P], f32r)
        cwl = a4.take("cwl", [P, 4, P], f32r)
        onesk = a4.take("onesk", [P, P])
        a5 = Area(x0, w0)
        woh = a5.take("woh", [P, KD, D], f32r)
        wol = a5.take("wol", [P, KD, D], f32r)
        z1 = a5.off
        zh = a5.take("zh", [P, 2, KD, CH], f32r)
        zl = a5.take("zl", [P, 2, KD, CH], f32r)
        zsize = 4 * KD * CH
        wg = [at("wg0", [P, KD, CH], z1 + zsize), at("wg1", [P, KD, CH], z1 + 3 * zsize)]
        ab = Area(w0, r0)
        wor = ab.take("wor", [P, 2, D])
        yb = ab.take("yb", [P, 3, CH])
        gb = ab.take("gb", [P, 3, CH])
        crep = ab.take("crep", [P, KD, P])
        a6 = Area(r0, end)
        xres = a6.take("xres", [P, 2, D])
        tout = a6.take("tout", [P, 2, D])
        sqj = a6.take("sqj", [P, D])
        gbc = a6.take("gbc", [P, D])
        gpo = a6.take("gpo", [P, D])
        posr2 = a6.take("posr2", [P, 2, CH])
        posc2 = a6.take("posc2", [P, CH])

        def col(i, n=1):
            return sml[:, i:i + n]
        cs = col(0, 16)
        mo = 16
        kn, kp, k2 = col(48, 8), col(56, 8), col(64, 8)
        epsc, lnepsc = col(72), col(73)
        sq2 = col(74, 8)
        ssq = col(82, 4)
        rst = col(86, 8)
        carry = col(94, 2)
        lt = col(96, 32)
        ss2, ssum, rs2, rr2 = lt[:, 0:2], lt[:, 2:3], lt[:, 3:4], lt[:, 4:5]

        def par_col(name, i=0, n=1):
            return prm[:, PAR[name] + i:PAR[name] + i + n]

        bank = [es.enter_context(nc.psum_tensor(f"bank{i}", [P, CH], f32)) for i in range(8)]
        pu = bank[0:2]
        gr = [bank[2:4], bank[6:8]]
        gi_ = bank[4:6]
        tp = bank[4:8]
        junk = bank[2:4]
        lmu, lvar, lpo, pmb = bank[2], bank[3], bank[4:6], bank[6:8]
        ob = [bank[2:4], bank[4:6], bank[6:8]]
        gob = bank[0:2]

        def sem(name):
            return es.enter_context(nc.semaphore(name))

        s_par, s_id, s_posc = sem("params_in"), sem("ident_ready"), sem("poscol_in")
        s_wm = [sem(f"wmod_in{m}") for m in range(8)]
        s_mrow, s_modT = sem("mod_rows"), sem("mod_turned")
        s_cs, s_mod, s_sc, s_kl = sem("silu_c"), sem("mod_psum"), sem("scales_ready"), sem("lru_consts")
        s_xin = [sem(f"x_in{g}") for g in range(NCH + 1)]
        s_pr, s_pad, s_pcd = sem("posrow_in"), sem("posrow_added"), sem("poscol_added")
        s_sqh, s_ssum, s_el = sem("squares_half"), sem("square_sums"), sem("exp_lam")
        s_oss = sem("out_square_sum")
        s_sq, s_sd, s_xh = sem("squares"), sem("rms_root"), sem("xhat_ready")
        s_tp, s_f, s_hh, s_hl = sem("transposed"), sem("modulated"), sem("hT_hi"), sem("hT_lo")
        s_wr, s_whi, s_wlo = sem("w_raw_in"), sem("w_hi"), sem("w_lo")
        s_pu, s_ev = sem("unit_done"), sem("unit_evacuated")
        s_us = [sem(f"u_stored{b}") for b in range(2)]
        s_gz, s_gw, s_gwh, s_gwl = sem("gatew_zeroed"), sem("gatew_in"), sem("gatew_hi"), sem("gatew_lo")
        s_v, s_cv = [sem(f"v_in{b}") for b in range(2)], sem("convolved")
        s_sh, s_sl, s_pg, s_sig = sem("split_hi"), sem("split_lo"), sem("gates_done"), sem("sigmoids")
        s_aq, s_exp, s_m2, s_rt = sem("a_and_q"), sem("tanhs"), sem("one_minus_a2"), sem("roots")
        s_ix, s_st, s_ya, s_ys = sem("gated_input"), sem("scan_done"), sem("y_added"), sem("y_stored")
        s_cgs, s_ct = sem("conf_sigmoid"), sem("conf_taps")
        s_cl, s_cst = [sem(f"conf_in{b}") for b in range(2)], [sem(f"conf_stored{b}") for b in range(2)]
        s_dve = sem("dve_chain")
        s_pool = sem("pool_chain")
        s_tw, s_twz, s_twh, s_twl = sem("tailw_in"), sem("tailw_zero"), sem("tailw_hi"), sem("tailw_lo")
        s_la, s_mu, s_zc, s_lsq, s_var = sem("ln_in"), sem("ln_mean"), sem("ln_centred"), sem("ln_squares"), sem("ln_var")
        s_lsd, s_lzn, s_lsi, s_lhi, s_llo = sem("ln_root"), sem("ln_normed"), sem("ln_silu"), sem("ln_hi"), sem("ln_lo")
        s_lpw, s_lye, s_lys = sem("conf_product"), sem("conf_y"), sem("conf_y_stored")
        s_pa = sem("pair_sums")
        s_pvi, s_psm, s_pd, s_pdh, s_pdl = sem("pool_in"), sem("pool_sums"), sem("pool_diff"), sem("pool_hi"), sem("pool_lo")
        s_pmm, s_pye, s_pys = sem("pool_product"), sem("pool_y"), sem("pool_y_stored")
        s_wor, s_woh, s_wol = [sem(f"wo_in{b}") for b in range(2)], sem("wo_hi"), sem("wo_lo")
        s_cr, s_gmm, s_gbc, s_gpo = sem("c_repeated"), sem("gate_product"), sem("gate_row"), sem("gpost_in")
        s_wg = [sem(f"wgate_in{h}") for h in range(2)]
        s_yg = [sem(f"yg_in{b}") for b in range(3)]
        s_sg, s_z, s_zh, s_zl = sem("gate_silu"), sem("z_ready"), sem("z_hi"), sem("z_lo")
        s_om, s_osq, s_ort, s_ot = sem("out_product"), sem("out_squares"), sem("out_root"), sem("out_scaled")
        s_xr = [sem(f"xres_in{b}") for b in range(2)]
        s_xp, s_of = sem("xres_pos"), sem("out_final")
        s_out = [sem(f"out_stored{b}") for b in range(2)]
        s_p2c = sem("poscol2_in")

        block = es.enter_context(nc.Block())

        GROUPS = [("ctx", CTX // P)] + [(c, TPC) for c in range(NCH)]

        def tiles_before(g):
            return 0 if g == 0 else CTX // P + TPC * (g - 1)

        def group_cols(g):
            return (c3, c3 + CTX) if g == 0 else ((g - 1) * CH, g * CH)

        def rows(g, i, k0, k1):
            if g == 0:
                return cbuf[:, i, k0:k1, :]
            a = (g - 1) * CH + i * P
            return xg[:, k0:k1, a:a + P]

        def low_place(g, k):
            return hcl[:, k, :] if g == 0 else xTl[:, k, (g - 1) * CH:g * CH]

        def slices(ap):
            return ap.rearrange("p (k j) -> p k j", j=P)

        def early_w(t):
            if t < 2:
                return wh[:, t], wl[:, t]
            a = c3 + CTX + (t - 2) * P
            return xTh[:, :, a:a + P], ewl[:, t - 2]

        W_JOBS = [(t, early_w(t)) for t in range(4)] + [(ORDER[o], (wh[:, o % 2], wl[:, o % 2])) for o in range(2, NT_IN)]

        def w_slot_free(w):
            if w < 4:
                return 0
            o = w - 2 - 2
            return N_CU + max(n for n, (oo, c) in enumerate(UNITS) if oo == o) + 1

        def w_job_of(o):
            return o if o < 2 else o + 2

        def step_chunks(s):
            return (None, None) if s == 0 else (s - 1, NCH - s)

        def xc_piece(c):
            return xc[:, 0:CTX] if c is None or c == "ctx" else xc[:, CTX + c * CH:CTX + (c + 1) * CH]

        LN_JOBS = list(range(NCH))
        POOL_JOBS = [(i, c) for c in range(NCH) for i in (0, 1)]
        rest = [("unit", n) for n in range(GATES_AFTER[-1] + 1, len(UNITS))]
        TAIL, rest = rest[:-6], rest[-6:]
        side = [("gate", 0)] + [(kind, k) for k in range(KD) for kind in ("wo", "item")]
        side[9:9], side[14:14] = [("gmm", 0)], [("gmm", 1)]
        for c in range(NCH + 1):
            now, before = c < NCH, c > 0
            steps = [("mu", c) if now else None, ("swish", c - 1) if before else None,
                     ("pmm", 2 * c - 1) if before else None, rest.pop(0) if rest and now else None,
                     ("pool", 2 * c) if now else None,
                     rest.pop(0) if rest and now else None, ("var", c) if now else None, ("pw", c - 1) if before else None,
                     ("pool", 2 * c + 1) if now else None, ("pmm", 2 * c) if now else None,
                     rest.pop(0) if rest and now else None]
            for token in [token for token in steps if token]:
                TAIL.append(token)
                if ("unit", len(UNITS) - 1) in TAIL and token[0] in SIDE_BEHIND:
                    TAIL += side[:SIDE_PIECES]
                    side = side[SIDE_PIECES:]
        TAIL += side
        assert not rest
        ITEMS = [(c, k) for c in range(NCH) for k in range(KD)]
        TILES = [(c, i) for c in range(NCH) for i in range(TPC)]
        STAGE5 = []
        for n, (c, i) in enumerate(TILES):
            STAGE5.append(("tile", n))
            if c + 1 < NCH:
                STAGE5 += [("item", (c + 1) * KD + m) for m in range(3 * i, min(3 * i + 3, KD))]

        @block.sync
        def _(sp):
            sp.dma_start(prm[:], par).then_inc(s_par, 16)

            def load_rows(g):
                src = ctx if g == 0 else x[(g - 1) * CH:g * CH, :]
                for i in range(GROUPS[g][1]):
                    sp.dma_start(rows(g, i, 0, KD), src[i * P:(i + 1) * P, :].rearrange("p (k j) -> p k j", j=P)).then_inc(s_xin[g], 16)

            def load_pos(g):
                if g >= 2:
                    sp.wait_ge(s_pad, TPC * (g - 1))
                sp.dma_start(posr[:], pos_row[g - 1]).then_inc(s_pr, 16)

            def load_w(w):
                if w >= 1:
                    sp.wait_ge(s_wlo, w)
                sp.dma_start(wraw[:], w_in[W_JOBS[w][0]]).then_inc(s_wr, 16)

            def store_out(n):
                sp.wait_ge(s_of, n + 1)
                sp.dma_start(out[n * P:(n + 1) * P, :], tout[:, n % 2, :]).then_inc(s_out[n % 2], 16)

            for m in range(8):
                sp.dma_start(wm[:, m], w_mod[m]).then_inc(s_wm[m], 16)
                if m == 0:
                    load_w(0)
                if m == 1:
                    load_rows(0)
                if m == 3:
                    load_w(1)
                if m == 5:
                    load_rows(1)
                    load_pos(1)
                    sp.dma_start(posc[:], pos_col).then_inc(s_posc, 16)
            load_w(2)
            load_rows(2)
            load_pos(2)
            load_rows(3)
            load_w(3)
            load_rows(4)
            load_pos(3)

            def store_u(U):
                sp.wait_ge(s_ev, U + 1)
                if U < N_CU:
                    dst, n = uc_dram[U], CTX
                else:
                    o, c = UNITS[U - N_CU]
                    dst, n = u_dram[ORDER[o], :, c * CH:(c + 1) * CH], CH
                sp.dma_start(dst, ustage[:, U % 2, 0:n]).then_inc(s_us[U % 2], 16)

            for U in range(N_CU):
                store_u(U)
            for n in range(GATES_AFTER[-1] + 1):
                if n == 0:
                    load_pos(4)
                if n == 3:
                    load_w(4)
                store_u(N_CU + n)
                if n % 4 == 2 and n >= 6:
                    load_w((n + 2) // 4 + 3)

            def load_item(n):
                c, k = ITEMS[n]
                if n >= 3:
                    sp.wait_ge(s_zl, n - 2)
                if c == 0 and k == 4:
                    sp.wait_ge(s_pys, 32)
                if c == 0 and k == 6:
                    sp.wait_ge(s_lys, 32)
                sp.dma_start(yb[:, n % 3, :], y_dram[k, :, c * CH:(c + 1) * CH]).then_inc(s_yg[n % 3], 16)
                gt = (G_LRU + k) if k < 4 else (G_POOL + k - 4) if k < 6 else (G_CONF + k - 6)
                sp.dma_start(gb[:, n % 3, :], u_dram[gt, :, c * CH:(c + 1) * CH]).then_inc(s_yg[n % 3], 16)

            def load_wg(h):
                for m in range(2):
                    sp.dma_start(wg[h][:, :, m * 256:(m + 1) * 256], w_mod[8 + 2 * h + m]).then_inc(s_wg[h], 16)

            def load_wo(k):
                if k >= 2:
                    sp.wait_ge(s_wol, k - 1)
                sp.dma_start(wor[:, k % 2, :], w_out[k * P:(k + 1) * P, :]).then_inc(s_wor[k % 2], 16)

            for kind, n in TAIL:
                if kind == "gate":
                    sp.wait_ge(s_pu, N_CU + len(UNITS))
                    sp.wait_ge(s_wlo, len(W_JOBS))
                    sp.wait_ge(s_ys, 64 * N_LRU)
                    for b in range(2):
                        sp.wait_ge(s_us[b], 16 * (N_CU + len(UNITS)) // 2)
                    load_wo(0)
                    load_item(0)
                    load_wo(1)
                    load_item(1)
                    load_item(2)
                    load_wg(0)
                if kind == "wo" and n + 2 < KD:
                    load_wo(n + 2)
                if kind == "item" and n + 3 < KD:
                    load_item(n + 3)
                if kind == "item" and n == 0:
                    load_wg(1)
                if kind == "unit":
                    store_u(N_CU + n)
                    if n % 4 == 2 and (n + 2) // 4 + 3 < len(W_JOBS):
                        load_w((n + 2) // 4 + 3)
                if kind == "pmm":
                    i, c = POOL_JOBS[n]
                    sp.wait_ge(s_pye, n + 1)
                    sp.dma_start(y_dram[4 + i, :, c * CH:(c + 1) * CH], pyo[:]).then_inc(s_pys, 16)
                if kind == "pw":
                    sp.wait_ge(s_lye, 2 * n + 2)
                    for i in range(2):
                        sp.dma_start(y_dram[6 + i, :, n * CH:(n + 1) * CH], ly[:, i, :]).then_inc(s_lys, 16)

            sp.wait_ge(s_lye, 2 * NCH)
            sp.wait_ge(s_lys, 32 * NCH)
            sp.wait_ge(s_pys, 32 * NCH)
            sp.dma_start(gbc[:], b_gate.partition_broadcast(P)).then_inc(s_gpo, 16)
            sp.dma_start(gpo[:], g_post.partition_broadcast(P)).then_inc(s_gpo, 16)
            sp.dma_start(posc2[:], pos_col).then_inc(s_p2c, 16)
            for kind, n in STAGE5:
                if kind == "item":
                    load_item(n)
                else:
                    if n >= 2:
                        sp.wait_ge(s_of, n - 1)
                    sp.dma_start(xres[:, n % 2, :], x[n * P:(n + 1) * P, :]).then_inc(s_xr[n % 2], 16)
                    sp.dma_start(posr2[:, n % 2, :], pos_row[n // TPC, :, n % TPC, :]).then_inc(s_xr[n % 2], 16)
                    if n >= 1:
                        store_out(n - 1)
            store_out(len(TILES) - 1)
            for b in range(2):
                sp.wait_ge(s_out[b], 16 * len(TILES) // 2)

        @block.gpsimd
        def _(pool):
            g = nc.gpsimd

            def round_hi(dst, src):
                return g.tensor_scalar(dst, src, 1.0, 1.0, ALU.mult, ALU.mult)

            g.memset(ident[:], 0.0).then_inc(s_id, 1)
            pool.wait_ge(s_id, 1)
            g.affine_select(out=ident[:], in_=ident[:], compare_op=ALU.not_equal, fill=1.0, base=0,
                            pattern=[[-1, P]], channel_multiplier=1).then_inc(s_id, 1)

            def add_rows(gi):
                pool.wait_ge(s_xin[gi], 16 * TPC)
                pool.wait_ge(s_pr, 16 * gi)
                for i in range(TPC):
                    r = rows(gi, i, 0, KD // 2)
                    g.tensor_tensor(out=r, in0=r, in1=slices(posr[:, i, :]), op=ALU.add).then_inc(s_pad, 1)

            def hi_group(gi, ks=range(KD)):
                a, b = group_cols(gi)
                for k in ks:
                    idx = 8 * gi + k
                    pool.wait_ge(s_f, idx + 1)
                    if gi == NCH and k == 0:
                        pool.wait_ge(s_pu, N_CU)
                    round_hi(xTh[:, k, a:b], fbuf[:, idx % 4, 0:b - a]).then_inc(s_hh, 1)

            first, second = range(0, KD // 2), range(KD // 2, KD)
            add_rows(1)
            hi_group(0)
            hi_group(1, first)
            add_rows(2)
            hi_group(1, second)
            add_rows(3)
            for gi in range(2, NCH + 1):
                hi_group(gi, first)
                if gi + 2 <= NCH:
                    add_rows(gi + 2)
                hi_group(gi, second)
            pool.wait_ge(s_hl, 8 * (NCH + 1))
            g.memset(gwh[:].bitcast(f32), 0.0).then_inc(s_gz, 1)
            g.memset(gwl[:].bitcast(f32), 0.0).then_inc(s_gz, 1)

            def load_gate_w(t):
                if t:
                    pool.wait_ge(s_gwl, 2 * t)
                g.dma_start(gwr[:], gate_w[t]).then_inc(s_gw, 16)

            def load_v(p):
                t, j = divmod(p, NCH + 1)
                if p >= 2:
                    pool.wait_ge(s_cv, p - 1)
                c = PIECES[j]
                if c == "ctx":
                    pool.wait_ge(s_us[t % 2], 16 * (t // 2 + 1))
                    g.dma_start(vbuf[:, p % 2, 2:2 + CTX], uc_dram[t]).then_inc(s_v[p % 2], 16)
                else:
                    a, b = max(c * CH - 2, 0), min((c + 1) * CH + 1, SEQ)
                    U = unit_of(V_LRU + t, NCH - 1)
                    for back in (0, 1):
                        pool.wait_ge(s_us[(U - back) % 2], 16 * ((U - back) // 2 + 1))
                    off = a - (c * CH - 2)
                    g.dma_start(vbuf[:, p % 2, off:off + b - a], u_dram[V_LRU + t, :, a:b]).then_inc(s_v[p % 2], 16)

            def gate_w_hi(t):
                pool.wait_ge(s_gw, 16 * (t + 1))
                if t:
                    pool.wait_ge(s_pg, (NCH + 1) * t)
                else:
                    pool.wait_ge(s_gz, 2)
                for i, h in enumerate((slice(0, 64), slice(64, 128))):
                    round_hi(gwh[h, :, h], gwr[h]).then_inc(s_gwh, 1)
                    pool.wait_ge(s_gwh, 2 * t + i + 1)

            def split(q):
                t, s = divmod(q, NCH + 1)
                pool.wait_ge(s_cv, (NCH + 1) * t + LAST_PIECE[s] + 1)
                if q:
                    pool.wait_ge(s_pg, q)
                n = CTX if s == 0 else CH
                pieces = step_chunks(s)[0:1] if s == 0 else step_chunks(s)
                for d, c in enumerate(pieces):
                    round_hi(sph[:, d, 0:n], xc_piece(c)).then_inc(s_sh, 1)
                for d, c in enumerate(pieces):
                    pool.wait_ge(s_sh, splits_before(q) + d + 1)
                    g.tensor_tensor(out=spl[:, d, 0:n], in0=xc_piece(c), in1=sph[:, d, 0:n].bitcast(f32),
                                    op=ALU.subtract).then_inc(s_sl, 1)

            def gated_input(q):
                s = q % (NCH + 1)
                f, b = step_chunks(s)
                n = CTX if s == 0 else CH
                for d, c in enumerate((f, b)):
                    pool.wait_ge(s_sig, 4 * q + d + 3)
                    I = Ib[:, d, 0:n]
                    g.tensor_tensor(out=I, in0=I, in1=xc_piece(c), op=ALU.mult).then_inc(s_ix, 1)

            def add_y(q):
                t, s = divmod(q, NCH + 1)
                if s < 3:
                    return
                for d, c in enumerate(step_chunks(s)):
                    pool.wait_ge(s_st, 2 * q + d + 1)
                    yc = yrow[:, c * CH:(c + 1) * CH]
                    g.tensor_tensor(out=yc, in0=yc, in1=Qb[:, d, :], op=ALU.add).then_inc(s_ya, 1)
                pool.wait_ge(s_ya, 4 * t + 2 * (s - 3) + 2)
                for c in step_chunks(s):
                    g.dma_start(y_dram[t, :, c * CH:(c + 1) * CH], yrow[:, c * CH:(c + 1) * CH]).then_inc(s_ys, 16)

            def load_conf(j):
                i, c = CONF_JOBS[j]
                cz, cg = czb[:, j % 2, :], cgb[:, j % 2, :]
                if j >= 2:
                    pool.wait_ge(s_cst[j % 2], 16 * (j // 2))
                for tile in (V_CONF + i, GG_CONF + i):
                    U = unit_of(tile, min(c + 1, NCH - 1))
                    for back in (0, 1):
                        pool.wait_ge(s_us[(U - back) % 2], 16 * ((U - back) // 2 + 1))
                a, b = max(c * CH - HALO, 0), min((c + 1) * CH + HALO, SEQ)
                off = a - (c * CH - HALO)
                g.dma_start(cz[:, off:off + b - a], u_dram[V_CONF + i, :, a:b]).then_inc(s_cl[j % 2], 16)
                g.dma_start(cg[:, off:off + b - a], u_dram[GG_CONF + i, :, a:b]).then_inc(s_cl[j % 2], 16)

            def store_conf(j):
                i, c = CONF_JOBS[j]
                pool.wait_ge(s_ct, j + 1)
                g.dma_start(cv_dram[i, :, c * CH:(c + 1) * CH], cgb[:, j % 2, 0:CH]).then_inc(s_cst[j % 2], 16)

            def w_lo(w):
                pool.wait_ge(s_whi, w + 1)
                h, l = W_JOBS[w][1]
                g.tensor_tensor(out=l, in0=wraw[:], in1=h.bitcast(f32), op=ALU.subtract).then_inc(s_wlo, 1)

            load_gate_w(0)
            load_v(0)
            w_lo(4)
            load_v(1)
            gate_w_hi(0)
            split(0)
            load_v(2)
            load_v(3)
            done_w = 5
            for q in range(STEPS):
                t, s = divmod(q, NCH + 1)
                more = t + 1 < N_LRU
                here, after = (NCH + 1) * t, (NCH + 1) * (t + 1)
                if s == NCH and more:
                    gate_w_hi(t + 1)
                if s == 1:
                    load_v(here + 4)
                if q + 1 < STEPS:
                    split(q + 1)
                if s == 2 and more:
                    load_gate_w(t + 1)
                    load_v(after)
                if s == NCH and more:
                    load_v(after + 2)
                gated_input(q)
                upto = GATES_AFTER[q + 1] if q + 1 < STEPS else GATES_AFTER[-1] + 1
                while done_w < len(W_JOBS) and 4 * (done_w - 3) < upto:
                    w_lo(done_w)
                    done_w += 1
                if s == 3 and more:
                    load_v(after + 1)
                for j in range(len(CONF_JOBS)):
                    if JOB_LOAD[j] == q:
                        load_conf(j)
                add_y(q)
                if s == NCH and more:
                    load_v(after + 3)
                for j in range(len(CONF_JOBS)):
                    if JOB_LAST[j] == q:
                        store_conf(j)

            pool.wait_ge(s_ys, 64 * N_LRU)
            for b in range(2):
                pool.wait_ge(s_cst[b], 16 * len(CONF_JOBS) // 2)
            g.memset(pwr[:], 0.0).then_inc(s_twz, 1)
            g.memset(onesk[:], 1.0 / 256.0).then_inc(s_twz, 1)
            pool.wait_ge(s_twz, 1)
            for h in range(2):
                g.dma_start(pwr[64 * h:64 * h + 64, :, 64 * h:64 * h + 64], pool_w[h]).then_inc(s_tw, 16)
            g.dma_start(cwr[:], conf_pw).then_inc(s_tw, 16)
            pool.wait_ge(s_tw, 48)
            round_hi(pwh[:], pwr[:]).then_inc(s_twh, 1)
            round_hi(cwh[:], cwr[:]).then_inc(s_twh, 1)

            W2 = CH + 2 * PH

            def load_pool(n):
                i, c = POOL_JOBS[n]
                if n:
                    pool.wait_ge(s_pd, n)
                U = unit_of(V_POOL + i, NCH - 1)
                for back in (0, 1):
                    pool.wait_ge(s_us[(U - back) % 2], 16 * ((U - back) // 2 + 1))
                a, b = max(c * CH - PH, 0), min((c + 1) * CH + PH, SEQ)
                off = a - (c * CH - PH)
                if c == 0:
                    g.memset(pv[:, 0:PH], 0.0).then_inc(s_pool, 1)
                if c == NCH - 1:
                    g.memset(pv[:, PH + CH:], 0.0).then_inc(s_pool, 1)
                g.dma_start(pv[:, off:off + b - a], u_dram[V_POOL + i, :, a:b]).then_inc(s_pvi, 16)

            def load_ln(n):
                if n:
                    pool.wait_ge(s_zc, 2 * n)
                g.dma_start(la[:], cv_dram[:, :, n * CH:(n + 1) * CH].rearrange("i p n -> p i n")).then_inc(s_la, 16)

            def zero_waits(n):
                return sum((c == 0) + (c == NCH - 1) for i, c in POOL_JOBS[:n + 1])

            def pool_sums(n):
                pool.wait_ge(s_pool, zero_waits(n))
                pool.wait_ge(s_pvi, 16 * (n + 1))
                h = slice(64, 128)
                g.tensor_tensor(out=pa[:, 0:W2 - 1], in0=pv[:, 0:W2 - 1], in1=pv[:, 1:W2], op=ALU.add).then_inc(s_pa, 1)
                pool.wait_ge(s_pa, n // 2 + 1)
                g.tensor_tensor(out=pb[h, 0:W2 - 3], in0=pa[h, 0:W2 - 3], in1=pa[h, 2:W2 - 1], op=ALU.add).then_inc(s_psm, 1)
                pool.wait_ge(s_psm, n // 2 + 1)

            def pool_hi(n):
                pool.wait_ge(s_pd, n + 1)
                if n:
                    pool.wait_ge(s_pmm, n)
                round_hi(pdh[:], py[:]).then_inc(s_pdh, 1)

            def ln_hi(n):
                for m in range(2):
                    pool.wait_ge(s_lsi, 2 * n + m + 1)
                    if n and m == 0:
                        pool.wait_ge(s_lpw, 2 * n)
                    round_hi(lsh[:, m, :], lr[:, n % 2, m, :]).then_inc(s_lhi, 1)

            def z_hi(n):
                c, k = ITEMS[n]
                pool.wait_ge(s_z, n + 1)
                if n == KD:
                    pool.wait_ge(s_gmm, 2)
                if c >= 2 and k == 0:
                    pool.wait_ge(s_om, TPC * (c - 1))
                round_hi(zh[:, c % 2, k, :], yb[:, n % 3, :]).then_inc(s_zh, 1)

            load_ln(0)
            load_pool(0)
            for kind, n in TAIL:
                if kind == "unit" and n % 4 == 0 and done_w < len(W_JOBS):
                    w_lo(done_w)
                    done_w += 1
                if kind == "mu":
                    pool_sums(2 * n)
                    if n + 1 < NCH:
                        load_ln(n + 1)
                if kind == "pool":
                    pool_hi(n)
                    if n + 1 < len(POOL_JOBS):
                        load_pool(n + 1)
                if kind == "swish":
                    ln_hi(n)
                if kind == "item":
                    z_hi(n)

            for kind, n in STAGE5:
                if kind == "item":
                    z_hi(n)
                else:
                    pool.wait_ge(s_xr[n % 2], 32 * (n // 2 + 1))
                    if n == 0:
                        pool.wait_ge(s_p2c, 16)
                    g.tensor_tensor(out=xres[:, n % 2, 0:CH], in0=xres[:, n % 2, 0:CH], in1=posr2[:, n % 2, :],
                                    op=ALU.add).then_inc(s_xp, 1)
                    g.tensor_tensor(out=xres[:, n % 2, CH:D], in0=xres[:, n % 2, CH:D], in1=posc2[:],
                                    op=ALU.add).then_inc(s_xp, 1)

        @block.scalar
        def _(act):
            a = nc.scalar
            act.wait_ge(s_par, 16)
            a.activation(cs, par_col("c", 0, 16), ACT.Silu).then_inc(s_cs, 1)
            a.activation(lt[:, 0:8], par_col("lam", 0, 8), ACT.Abs).then_inc(s_el, 1)
            act.wait_ge(s_el, 1)
            a.activation(lt[:, 8:16], lt[:, 0:8], ACT.Exp, scale=-1.0).then_inc(s_el, 1)

            def w_hi(w):
                act.wait_ge(s_wr, 16 * (w + 1))
                if w_slot_free(w):
                    act.wait_ge(s_pu, w_slot_free(w))
                if w in (2, 3):
                    act.wait_ge(s_mod, 8)
                a.activation(W_JOBS[w][1][0], wraw[:], ACT.Copy).then_inc(s_whi, 1)

            def squares(gi):
                for i in range(GROUPS[gi][1]):
                    T = tiles_before(gi) + i
                    if gi == 0:
                        if i == 0:
                            act.wait_ge(s_xin[0], 16 * (CTX // P))
                    else:
                        act.wait_ge(s_pad, TPC * (gi - 1) + i + 1)
                        act.wait_ge(s_pcd, TPC * (gi - 1) + i + 1)
                    if T:
                        act.wait_ge(s_sq, T)
                        act.wait_ge(s_sqh, T)
                    if i == 0 and gi:
                        act.wait_ge(s_ssum, gi)
                    for h, done in ((0, s_sqh), (1, s_sq)):
                        a.activation(slices(junk[h][:]), rows(gi, i, 4 * h, 4 * h + 4), ACT.Square,
                                     accum_out=sq2[:, 2 * i + h:2 * i + h + 1]).then_inc(done, 1)

            def root(gi):
                act.wait_ge(s_ssum, gi + 1)
                n = GROUPS[gi][1]
                a.activation(rst[:, 0:n], ssq[:, 0:n], ACT.Sqrt, bias=epsc, scale=1.0 / D).then_inc(s_sd, 1)

            def modulate(gi, ks=range(KD)):
                n = GROUPS[gi][1] * P
                so = mo + (16 if gi == 0 else 0)
                for k in ks:
                    idx = 8 * gi + k
                    act.wait_ge(s_tp, idx + 1)
                    if idx >= 4:
                        act.wait_ge(s_hh, idx - 3)
                        act.wait_ge(s_hl, idx - 3)
                    a.activation(fbuf[:, idx % 4, 0:n], tp[idx % 4][:, 0:n], ACT.Identity,
                                 scale=col(so + k), bias=col(so + 8 + k)).then_inc(s_f, 1)

            def evac(U):
                act.wait_ge(s_pu, U + 1)
                if U >= 2:
                    act.wait_ge(s_us[U % 2], 16 * (U // 2))
                n = CTX if U < N_CU else CH
                a.activation(ustage[:, U % 2, 0:n], pu[U % 2][:, 0:n], ACT.Copy).then_inc(s_ev, 1)

            def sigmoids(q):
                t, s = divmod(q, NCH + 1)
                n = CTX if s == 0 else CH
                act.wait_ge(s_pg, q + 1)
                for d in range(2):
                    r = gr[q % 2][d][:, 0:n]
                    a.activation(r, r, ACT.Sigmoid, bias=par_col("lru_ba", 4 * d + t)).then_inc(s_sig, 1)
                for d in range(2):
                    if q:
                        act.wait_ge(s_st, 2 * (q - 1) + d + 1)
                    a.activation(Ib[:, d, 0:n], gi_[d][:, 0:n], ACT.Sigmoid,
                                 bias=par_col("lru_bx", 4 * d + t)).then_inc(s_sig, 1)

            def decays(q):
                t, s = divmod(q, NCH + 1)
                n = CTX if s == 0 else CH
                for d in range(2):
                    kc = 4 * d + t
                    act.wait_ge(s_sig, 4 * q + d + 1)
                    if s == 0 and t or s == 4:
                        act.wait_ge(s_ya, 4 * t if s == 0 else 4 * t + 2)
                    r = gr[q % 2][d][:, 0:n]
                    a.activation(Ab[:, d, 0:n], r, ACT.Exp, scale=kn[:, kc:kc + 1]).then_inc(s_aq, 1)
                    a.activation(Qb[:, d, 0:n], r, ACT.Exp, scale=k2[:, kc:kc + 1]).then_inc(s_aq, 1)
                    a.activation(r, r, ACT.Tanh, scale=kp[:, kc:kc + 1]).then_inc(s_exp, 1)

            def roots(q):
                s = q % (NCH + 1)
                n = CTX if s == 0 else CH
                for d in range(2):
                    act.wait_ge(s_m2, 2 * q + d + 1)
                    r = gr[q % 2][d][:, 0:n]
                    a.activation(r, r, ACT.Sqrt).then_inc(s_rt, 1)

            def conf_sigmoid(j):
                i, c = CONF_JOBS[j]
                lo = HALO if c == 0 else 0
                hi = CH + HALO if c == NCH - 1 else CH + 2 * HALO
                act.wait_ge(s_cl[j % 2], 32 * (j // 2 + 1))
                cg = cgb[:, j % 2, :]
                a.activation(cg[:, lo:hi], cg[:, lo:hi], ACT.Sigmoid).then_inc(s_cgs, 1)

            first, second = range(0, KD // 2), range(KD // 2, KD)
            w_hi(0)
            squares(0)
            root(0)
            w_hi(1)
            squares(1)
            root(1)
            act.wait_ge(s_sc, 1)
            modulate(0)
            w_hi(2)
            modulate(1, first)
            evac(0)
            modulate(1, second)
            w_hi(3)
            squares(2)
            evac(1)
            root(2)
            evac(2)
            evac(3)
            for gi in range(1, NCH + 1):
                if gi < NCH:
                    modulate(gi + 1, first)
                if gi + 2 <= NCH:
                    squares(gi + 2)
                    root(gi + 2)
                evac(N_CU + 2 * gi - 2)
                if gi < NCH:
                    modulate(gi + 1, second)
                if gi == NCH:
                    w_hi(4)
                evac(N_CU + 2 * gi - 1)

            def unit_side(n):
                if n % 4 == 0 and n // 4 + 3 < len(W_JOBS):
                    w_hi(n // 4 + 3)
                evac(N_CU + n)

            n = 8
            for q in range(STEPS):
                sigmoids(q)
                for j in range(len(CONF_JOBS)):
                    if JOB_LOAD[j] + 1 == q:
                        conf_sigmoid(j)
                upto = GATES_AFTER[q + 1] if q + 1 < STEPS else GATES_AFTER[-1] + 1
                first = n
                while n < min(first + 1, upto):
                    unit_side(n)
                    n += 1
                decays(q)
                while n < min(first + 2, upto):
                    unit_side(n)
                    n += 1
                roots(q)
                while n < upto:
                    unit_side(n)
                    n += 1

            def pool_evac(m):
                i, c = POOL_JOBS[m]
                act.wait_ge(s_pmm, m + 1)
                if m:
                    act.wait_ge(s_pys, 16 * m)
                a.activation(pyo[:], pmb[m % 2][:], ACT.Copy, scale=par_col("pool_scale", i)).then_inc(s_pye, 1)

            def ln_squares(m):
                for i in range(2):
                    act.wait_ge(s_zc, 2 * m + i + 1)
                    if m and i == 0:
                        act.wait_ge(s_var, m)
                    a.activation(lq[:, i, :], lr[:, m % 2, i, :], ACT.Square).then_inc(s_lsq, 1)

            def ln_root(m):
                act.wait_ge(s_var, m + 1)
                if m:
                    act.wait_ge(s_lzn, 2 * m)
                a.activation(lsd[:], lvar[:], ACT.Sqrt, bias=lnepsc).then_inc(s_lsd, 1)

            def ln_swish(m):
                for i in range(2):
                    act.wait_ge(s_lzn, 2 * m + i + 1)
                    z = lr[:, m % 2, i, :]
                    a.activation(z, z, ACT.Silu, scale=par_col("ln_g", i),
                                 bias=par_col("ln_b", i)).then_inc(s_lsi, 1)

            def conf_evac(m):
                for i in range(2):
                    act.wait_ge(s_lpw, 2 * m + i + 1)
                    if m and i == 0:
                        act.wait_ge(s_lys, 32 * m)
                    a.activation(ly[:, i, :], lpo[i][:], ACT.Copy).then_inc(s_lye, 1)

            def out_weights_hi(k):
                act.wait_ge(s_wor[k % 2], 16 * (k // 2 + 1))
                if k == 0:
                    act.wait_ge(s_pu, N_CU + len(UNITS))
                a.activation(woh[:, k, :], wor[:, k % 2, :], ACT.Copy).then_inc(s_woh, 1)

            def gate_silu(m):
                act.wait_ge(s_yg[m % 3], 32 * (m // 3 + 1))
                a.activation(gb[:, m % 3, :], gb[:, m % 3, :], ACT.Silu).then_inc(s_sg, 1)

            for kind, m in TAIL:
                if kind == "unit":
                    unit_side(m)
                if kind == "mu":
                    ln_squares(m)
                if kind == "var":
                    ln_root(m)
                if kind == "swish":
                    ln_swish(m)
                if kind == "wo":
                    out_weights_hi(m)
                if kind == "item":
                    gate_silu(m)
                if kind == "pmm":
                    pool_evac(m)
                if kind == "pw":
                    conf_evac(m)

            for kind, m in STAGE5:
                if kind == "item":
                    gate_silu(m)
                else:
                    act.wait_ge(s_om, m + 1)
                    if m:
                        act.wait_ge(s_oss, m)
                        act.wait_ge(s_osq, 2 * m)
                    for h in range(2):
                        a.activation(sqj[:, h * CH:(h + 1) * CH], ob[m % 3][h][:], ACT.Square,
                                     accum_out=ss2[:, h:h + 1]).then_inc(s_osq, 1)
                    act.wait_ge(s_oss, m + 1)
                    if m:
                        act.wait_ge(s_ot, m)
                    a.activation(rs2, ssum, ACT.Sqrt, bias=epsc, scale=1.0 / D).then_inc(s_ort, 1)

        @block.vector
        def _(dve):
            v = nc.vector
            chain = [0]

            def link(ins):
                chain[0] += 1
                ins.then_inc(s_dve, 1)
                dve.wait_ge(s_dve, chain[0])

            def stt(out, in0, sc, in1, op0, op1):
                return v.scalar_tensor_tensor(out=out, in0=in0, scalar=sc, in1=in1, op0=op0, op1=op1)

            v.memset(epsc, EPS).then_inc(s_kl, 1)
            v.memset(lnepsc, LN_EPS).then_inc(s_kl, 1)
            dve.wait_ge(s_el, 2)
            e, y, y2, sr = lt[:, 8:16], lt[:, 0:8], lt[:, 16:24], lt[:, 24:32]
            link(v.tensor_scalar(y2, e, 2.0, None, ALU.add))
            link(v.reciprocal(y2, y2))
            link(v.tensor_tensor(out=y, in0=e, in1=y2, op=ALU.mult))
            link(v.tensor_tensor(out=y2, in0=y, in1=y, op=ALU.mult))
            link(v.tensor_scalar(sr, y2, 1.0 / 21.0, 1.0 / 19.0, ALU.mult, ALU.add))
            for j in range(17, 0, -2):
                link(v.tensor_tensor(out=sr, in0=sr, in1=y2, op=ALU.mult))
                link(v.tensor_scalar(sr, sr, 1.0 / j, None, ALU.add))
            link(v.tensor_tensor(out=sr, in0=sr, in1=y, op=ALU.mult))
            link(v.tensor_scalar(y, par_col("lam", 0, 8), -1.0, 0.0, ALU.mult, ALU.max))
            link(stt(sr, sr, 2.0, y, ALU.mult, ALU.add))
            link(v.tensor_scalar(kp, sr, 8.0, None, ALU.mult))
            link(v.tensor_scalar(k2, sr, -16.0, None, ALU.mult))
            v.tensor_scalar(kn, sr, -8.0, None, ALU.mult).then_inc(s_kl, 1)

            def w_lo(w):
                dve.wait_ge(s_whi, w + 1)
                h, l = W_JOBS[w][1]
                v.tensor_tensor(out=l, in0=wraw[:], in1=h.bitcast(f32), op=ALU.subtract).then_inc(s_wlo, 1)

            def add_cols(gi):
                dve.wait_ge(s_xin[gi], 16 * TPC)
                dve.wait_ge(s_posc, 16)
                for i in range(TPC):
                    r = rows(gi, i, KD // 2, KD)
                    v.tensor_tensor(out=r, in0=r, in1=slices(posc[:]), op=ALU.add).then_inc(s_pcd, 1)

            def normalise(gi):
                n = GROUPS[gi][1]
                dve.wait_ge(s_sq, tiles_before(gi) + n)
                v.tensor_tensor(out=ssq[:, 0:n], in0=sq2[:, 0:2 * n:2], in1=sq2[:, 1:2 * n:2], op=ALU.add).then_inc(s_ssum, 1)
                dve.wait_ge(s_sd, gi + 1)
                link(v.reciprocal(rst[:, 4:4 + n], rst[:, 0:n]))
                for i in range(n):
                    r = rows(gi, i, 0, KD)
                    ins = v.tensor_scalar(r, r, rst[:, 4 + i:5 + i], None, ALU.mult)
                ins.then_inc(s_xh, 1)

            def lo_group(gi, ks=range(KD)):
                a, b = group_cols(gi)
                for k in ks:
                    idx = 8 * gi + k
                    dve.wait_ge(s_hh, idx + 1)
                    v.tensor_tensor(out=low_place(gi, k), in0=fbuf[:, idx % 4, 0:b - a],
                                    in1=xTh[:, k, a:b].bitcast(f32), op=ALU.subtract).then_inc(s_hl, 1)

            def mod_rows(blocks):
                for m in blocks:
                    dve.wait_ge(s_mod, 2 * m + 2)
                    v.tensor_copy(mrow[:, m * CH:(m + 1) * CH], bank[4 + m][0:2, :]).then_inc(s_mrow, 1)

            def scales():
                dve.wait_ge(s_modT, 4)
                m = bank[0][:, 0:32].rearrange("p (m s) -> p s m", s=2)
                for s, off in ((0, mo), (1, mo + 16)):
                    link(stt(col(off, 8), m[:, s, 8:16], 1.0, par_col("b_mod", 8, 8), ALU.add, ALU.add))
                    link(v.tensor_tensor(out=col(off, 8), in0=col(off, 8), in1=par_col("g_pre", 0, 8), op=ALU.mult))
                    link(v.tensor_tensor(out=col(off + 8, 8), in0=m[:, s, 0:8], in1=par_col("b_mod", 0, 8), op=ALU.add))
                v.memset(carry, 0.0).then_inc(s_sc, 1)

            first, second = range(0, KD // 2), range(KD // 2, KD)
            w_lo(0)
            normalise(0)
            w_lo(1)
            mod_rows((0, 1))
            add_cols(1)
            normalise(1)
            mod_rows((2, 3))
            scales()
            lo_group(0)
            w_lo(2)
            lo_group(1, first)
            add_cols(2)
            lo_group(1, second)
            w_lo(3)
            normalise(2)
            add_cols(3)
            for gi in range(2, NCH + 1):
                lo_group(gi, first)
                if gi < NCH:
                    normalise(gi + 1)
                if gi + 2 <= NCH:
                    add_cols(gi + 2)
                lo_group(gi, second)

            def gate_w_lo(t):
                for i, h in enumerate((slice(0, 64), slice(64, 128))):
                    dve.wait_ge(s_gwh, 2 * t + i + 1)
                    v.tensor_tensor(out=gwl[h, :, h], in0=gwr[h], in1=gwh[h, :, h].bitcast(f32),
                                    op=ALU.subtract).then_inc(s_gwl, 1)

            def conv(p):
                t, j = divmod(p, NCH + 1)
                c = PIECES[j]
                n = CTX if c == "ctx" else CH
                dst = xc_piece(c)
                vb = vbuf[:, p % 2, :]
                if c in ("ctx", 0):
                    link(v.memset(vb[:, 0:2], 0.0))
                if c in ("ctx", NCH - 1):
                    link(v.memset(vb[:, 2 + n:3 + n], 0.0))
                dve.wait_ge(s_v[p % 2], 16 * (p // 2 + 1))
                if t:
                    dve.wait_ge(s_ix, 2 * ((NCH + 1) * (t - 1) + LAST_USE[j] + 1))
                w = [par_col("conv_w", 4 * t + i) for i in range(4)]
                link(v.tensor_scalar(dst, vb[:, 0:n], w[0], par_col("conv_b", t), ALU.mult, ALU.add))
                link(stt(dst, vb[:, 1:1 + n], w[1], dst, ALU.mult, ALU.add))
                link(stt(dst, vb[:, 2:2 + n], w[2], dst, ALU.mult, ALU.add))
                stt(dst, vb[:, 3:3 + n], w[3], dst, ALU.mult, ALU.add).then_inc(s_cv, 1)
                dve.wait_ge(s_cv, p + 1)

            def one_minus_a2(q):
                n = CTX if q % (NCH + 1) == 0 else CH
                for d in range(2):
                    dve.wait_ge(s_exp, 2 * q + d + 1)
                    r = gr[q % 2][d][:, 0:n]
                    stt(r, Qb[:, d, 0:n], 1.0, r, ALU.add, ALU.mult).then_inc(s_m2, 1)

            def scans(q):
                t, s = divmod(q, NCH + 1)
                n = CTX if s == 0 else CH
                for d, c in enumerate(step_chunks(s)):
                    dve.wait_ge(s_rt, 2 * q + d + 1)
                    dve.wait_ge(s_ix, 2 * q + d + 1)
                    I = Ib[:, d, 0:n]
                    link(v.tensor_tensor(out=I, in0=I, in1=gr[q % 2][d][:, 0:n], op=ALU.mult))
                    if s in (1, 2):
                        if t:
                            dve.wait_ge(s_ys, 64 * t)
                        o = yrow[:, c * CH:(c + 1) * CH]
                    else:
                        o = Qb[:, d, 0:n]
                    A, B, O = Ab[:, d, 0:n], I, o
                    if d:
                        A, B, O = A[:, ::-1], B[:, ::-1], o[:, ::-1]
                    ins = v.tensor_tensor_scan(out=O, data0=A, data1=B, initial=0.0 if s == 0 else carry[:, d:d + 1],
                                               op0=ALU.mult, op1=ALU.add)
                    if s == NCH:
                        ins.then_inc(s_st, 1)
                    else:
                        link(ins)
                        last = o[:, 0:1] if d else o[:, n - 1:n]
                        v.tensor_copy(carry[:, d:d + 1], last).then_inc(s_st, 1)
                        dve.wait_ge(s_st, 2 * q + d + 1)

            def glu(j):
                i, c = CONF_JOBS[j]
                lo = HALO if c == 0 else 0
                hi = CH + HALO if c == NCH - 1 else CH + 2 * HALO
                dve.wait_ge(s_cgs, j + 1)
                cz, cg = czb[:, j % 2, :], cgb[:, j % 2, :]
                link(v.tensor_tensor(out=cz[:, lo:hi], in0=cz[:, lo:hi], in1=cg[:, lo:hi], op=ALU.mult))
                if c == 0:
                    link(v.memset(cz[:, 0:HALO], 0.0))
                if c == NCH - 1:
                    link(v.memset(cz[:, CH + HALO:], 0.0))

            def tap(j, k):
                if k == 0:
                    glu(j)
                i, c = CONF_JOBS[j]
                cz, acc = czb[:, j % 2, :], cgb[:, j % 2, 0:CH]
                w = par_col("conf_dw", CONF_K * i + k)
                if k == 0:
                    link(v.tensor_scalar(acc, cz[:, 0:CH], w, par_col("conf_dw_b", i), ALU.mult, ALU.add))
                elif k < CONF_K - 1:
                    link(stt(acc, cz[:, k:k + CH], w, acc, ALU.mult, ALU.add))
                else:
                    stt(acc, cz[:, k:k + CH], w, acc, ALU.mult, ALU.add).then_inc(s_ct, 1)

            conv(0)
            gate_w_lo(0)
            conv(1)
            for q in range(STEPS):
                t, s = divmod(q, NCH + 1)
                here, after = (NCH + 1) * t, (NCH + 1) * (t + 1)
                if s == 0:
                    conv(here + 2)
                    conv(here + 3)
                if s == 1:
                    conv(here + 4)
                behind = min(TAPS_BEHIND, len(TAP_PLAN[q]))
                ahead = len(TAP_PLAN[q]) - behind
                for j, k in TAP_PLAN[q][:ahead]:
                    tap(j, k)
                if s == NCH and t + 1 < N_LRU:
                    gate_w_lo(t + 1)
                one_minus_a2(q)
                for j, k in TAP_PLAN[q][ahead:]:
                    tap(j, k)
                scans(q)
                if s == NCH - 1 and t + 1 < N_LRU:
                    conv(after)
                if s == NCH and t + 1 < N_LRU:
                    conv(after + 1)

            dve.wait_ge(s_twh, 2)
            v.tensor_tensor(out=pwl[:], in0=pwr[:], in1=pwh[:].bitcast(f32), op=ALU.subtract).then_inc(s_twl, 1)
            v.tensor_tensor(out=cwl[:], in0=cwr[:], in1=cwh[:].bitcast(f32), op=ALU.subtract).then_inc(s_twl, 1)

            def pool_diff(n):
                i, c = POOL_JOBS[n]
                if i == 0:
                    dve.wait_ge(s_psm, n // 2 + 1)
                else:
                    W2, up, add = CH + 2 * PH, slice(64, 128), ALU.add
                    dve.wait_ge(s_pool, sum((cc == 0) + (cc == NCH - 1) for ii, cc in POOL_JOBS[:n + 1]))
                    dve.wait_ge(s_pvi, 16 * (n + 1))
                    link(v.tensor_tensor(out=pa[:, 0:W2 - 1], in0=pv[:, 0:W2 - 1], in1=pv[:, 1:W2], op=add))
                    link(v.tensor_tensor(out=pb[:, 0:W2 - 3], in0=pa[:, 0:W2 - 3], in1=pa[:, 2:W2 - 1], op=add))
                    link(v.tensor_tensor(out=pa[:, 0:W2 - 7], in0=pb[:, 0:W2 - 7], in1=pb[:, 4:W2 - 3], op=add))
                    link(v.tensor_tensor(out=pb[up, 0:W2 - 15], in0=pa[up, 0:W2 - 15], in1=pa[up, 8:W2 - 7], op=add))
                if n:
                    dve.wait_ge(s_pdh, n)
                    dve.wait_ge(s_pdl, n)
                w_lo_, w_hi_ = (2, 4) if i == 0 else (8, 16)
                for h, w, src in ((slice(0, 64), w_lo_, pa), (slice(64, 128), w_hi_, pb)):
                    o = PH - w // 2
                    if c == 0:
                        link(v.tensor_tensor(out=src[h, o:o + 8], in0=src[h, o:o + 8],
                                             in1=prm[h, PAR["pool_edge"] + 16 * i:PAR["pool_edge"] + 16 * i + 8], op=ALU.mult))
                    if c == NCH - 1:
                        link(v.tensor_tensor(out=src[h, o + CH - 8:o + CH], in0=src[h, o + CH - 8:o + CH],
                                             in1=prm[h, PAR["pool_edge"] + 16 * i + 8:PAR["pool_edge"] + 16 * i + 16], op=ALU.mult))
                    ins = stt(py[h, :], src[h, o:o + CH], 1.0 / w, pv[h, PH:PH + CH], ALU.mult, ALU.subtract)
                ins.then_inc(s_pd, 1)
                dve.wait_ge(s_pdh, n + 1)
                v.tensor_tensor(out=pdl[:], in0=py[:], in1=pdh[:].bitcast(f32), op=ALU.subtract).then_inc(s_pdl, 1)

            def ln_centre(n):
                dve.wait_ge(s_mu, n + 1)
                for i in range(2):
                    v.tensor_tensor(out=lr[:, n % 2, i, :], in0=la[:, i, :], in1=lmu[:], op=ALU.subtract).then_inc(s_zc, 1)

            def ln_norm(n):
                dve.wait_ge(s_lsd, n + 1)
                link(v.reciprocal(lsd[:], lsd[:]))
                for i in range(2):
                    z = lr[:, n % 2, i, :]
                    v.tensor_tensor(out=z, in0=z, in1=lsd[:], op=ALU.mult).then_inc(s_lzn, 1)

            def ln_lo(n):
                for i in range(2):
                    dve.wait_ge(s_lhi, 2 * n + i + 1)
                    v.tensor_tensor(out=lsl[:, i, :], in0=lr[:, n % 2, i, :], in1=lsh[:, i, :].bitcast(f32),
                                    op=ALU.subtract).then_inc(s_llo, 1)

            def out_weights_lo(k):
                dve.wait_ge(s_woh, k + 1)
                v.tensor_tensor(out=wol[:, k, :], in0=wor[:, k % 2, :], in1=woh[:, k, :].bitcast(f32),
                                op=ALU.subtract).then_inc(s_wol, 1)

            def z_item(n):
                c, k = ITEMS[n]
                dve.wait_ge(s_sg, n + 1)
                z = yb[:, n % 3, :]
                v.tensor_tensor(out=z, in0=z, in1=gb[:, n % 3, :], op=ALU.mult).then_inc(s_z, 1)
                dve.wait_ge(s_zh, n + 1)
                v.tensor_tensor(out=zl[:, c % 2, k, :], in0=z, in1=zh[:, c % 2, k, :].bitcast(f32),
                                op=ALU.subtract).then_inc(s_zl, 1)

            for kind, n in TAIL:
                if kind == "pool":
                    pool_diff(n)
                if kind == "mu":
                    ln_centre(n)
                if kind == "var":
                    ln_norm(n)
                if kind == "swish":
                    ln_lo(n)
                if kind == "gate":
                    for b in range(2):
                        dve.wait_ge(s_us[b], 16 * (N_CU + len(UNITS)) // 2)
                    v.tensor_copy(crep[:], cs[:, 0:16:2].unsqueeze(2).to_broadcast([P, KD, P])).then_inc(s_cr, 1)
                if kind == "wo":
                    out_weights_lo(n)
                if kind == "item":
                    z_item(n)

            dve.wait_ge(s_gpo, 32)
            dve.wait_ge(s_gmm, 2)
            for h in range(2):
                hs = slice(h * CH, (h + 1) * CH)
                link(v.tensor_tensor(out=gbc[:, hs], in0=gbc[:, hs], in1=gob[h][:], op=ALU.add))
                link(v.tensor_tensor(out=gbc[:, hs], in0=gbc[:, hs], in1=gpo[:, hs], op=ALU.mult))
            for kind, n in STAGE5:
                if kind == "item":
                    z_item(n)
                else:
                    dve.wait_ge(s_osq, 2 * n + 2)
                    v.tensor_tensor(out=ssum, in0=ss2[:, 0:1], in1=ss2[:, 1:2], op=ALU.add).then_inc(s_oss, 1)
                    dve.wait_ge(s_ort, n + 1)
                    link(v.reciprocal(rr2, rs2))
                    if n >= 2:
                        dve.wait_ge(s_out[n % 2], 16 * (n // 2))
                    for h in range(2):
                        hs = slice(h * CH, (h + 1) * CH)
                        ins = stt(tout[:, n % 2, hs], ob[n % 3][h][:], rr2, gbc[:, hs], ALU.mult, ALU.mult)
                    ins.then_inc(s_ot, 1)
                    dve.wait_ge(s_ot, n + 1)
                    dve.wait_ge(s_xp, 2 * n + 2)
                    v.tensor_tensor(out=tout[:, n % 2, :], in0=tout[:, n % 2, :], in1=xres[:, n % 2, :],
                                    op=ALU.add).then_inc(s_of, 1)

        @block.tensor
        def _(pe):
            mm = nc.tensor.matmul

            def mm3(out, wh_, wl_, xh_, xl_, first, last):
                mm(out, wh_, xh_, start=first, stop=False)
                mm(out, wh_, xl_, start=False, stop=False)
                return mm(out, wl_, xh_, start=False, stop=last)

            pe.wait_ge(s_cs, 1)
            for m in range(8):
                pe.wait_ge(s_wm[m], 16)
                for k in range(KD):
                    ins = mm(bank[4 + m // 2][0:2, (m % 2) * 256:(m % 2) * 256 + 256], cs[:, 2 * k:2 * k + 2],
                             wm[:, m, k, :], start=(k == 0), stop=(k == KD - 1))
                ins.then_inc(s_mod, 1)
            pe.wait_ge(s_id, 2)
            for m in range(4):
                pe.wait_ge(s_mrow, m + 1)
                for j in range(4):
                    mt = 4 * m + j
                    ins = nc.tensor.transpose(bank[0][:, 2 * mt:2 * mt + 2], mrow[:, mt * P:(mt + 1) * P], ident[0:2, 0:2])
                ins.then_inc(s_modT, 1)

            def transposes(gi, ks=range(KD)):
                pe.wait_ge(s_xh, gi + 1)
                if gi == 0:
                    pe.wait_ge(s_id, 2)
                for k in ks:
                    idx = 8 * gi + k
                    if idx >= 4:
                        pe.wait_ge(s_f, idx - 3)
                    for i in range(GROUPS[gi][1]):
                        ins = nc.tensor.transpose(tp[idx % 4][:, i * P:(i + 1) * P],
                                                  rows(gi, i, k, k + 1)[:, 0, :], ident[:])
                    ins.then_inc(s_tp, 1)

            def project(U, h, l, xh, xl, n):
                if U >= 2:
                    pe.wait_ge(s_ev, U - 1)
                for k in range(KD):
                    ins = mm3(pu[U % 2][:, 0:n], h[:, k, :], l[:, k, :], xh[:, k], xl[:, k], k == 0, k == KD - 1)
                ins.then_inc(s_pu, 1)

            def unit(n):
                o, c = UNITS[n]
                w = w_job_of(o)
                pe.wait_ge(s_wlo, w + 1)
                pe.wait_ge(s_hl, 8 * (c + 2))
                cols = slice(c * CH, (c + 1) * CH)
                project(N_CU + n, wh[:, o % 2], wl[:, o % 2], xTh[:, :, cols], xTl[:, :, cols], CH)

            def gates(q):
                t, s = divmod(q, NCH + 1)
                n = CTX if s == 0 else CH
                if s == 0:
                    pe.wait_ge(s_gwl, 2 * t + 2)
                pe.wait_ge(s_sl, splits_before(q + 1))
                if q:
                    pe.wait_ge(s_sig, 4 * q)
                if q >= 2:
                    pe.wait_ge(s_st, 2 * (q - 1))
                for m in range(4):
                    d = 0 if s == 0 else m // 2
                    b = gi_[m // 2] if m % 2 else gr[q % 2][m // 2]
                    ins = mm3(b[:, 0:n], gwh[:, m, :], gwl[:, m, :], sph[:, d, 0:n], spl[:, d, 0:n], True, True)
                ins.then_inc(s_pg, 1)

            first, second = range(0, KD // 2), range(KD // 2, KD)
            transposes(0)
            transposes(1, first)
            pe.wait_ge(s_sc, 1)
            pe.wait_ge(s_hl, 8)
            for U in range(N_CU):
                pe.wait_ge(s_wlo, U + 1)
                h, l = early_w(U)
                project(U, h, l, xTh[:, :, c3:c3 + CTX], hcl[:], CTX)
                if U == 0:
                    transposes(1, second)
            for gi in range(1, NCH + 1):
                if gi < NCH:
                    transposes(gi + 1, first)
                unit(2 * gi - 2)
                if gi < NCH:
                    transposes(gi + 1, second)
                unit(2 * gi - 1)
            q = 0
            for n in range(8, GATES_AFTER[-1] + 1):
                unit(n)
                if q < STEPS and GATES_AFTER[q] == n:
                    gates(q)
                    q += 1
            assert q == STEPS
            for kind, n in TAIL:
                if kind == "unit":
                    unit(n)
                if kind == "mu":
                    pe.wait_ge(s_twz, 2)
                    pe.wait_ge(s_la, 16 * (n + 1))
                    if n:
                        pe.wait_ge(s_zc, 2 * n)
                    else:
                        pe.wait_ge(s_st, 2 * STEPS)
                    for i in range(2):
                        ins = mm(lmu[:], onesk[:], la[:, i, :], start=(i == 0), stop=(i == 1))
                    ins.then_inc(s_mu, 1)
                if kind == "var":
                    pe.wait_ge(s_lsq, 2 * n + 2)
                    if n:
                        pe.wait_ge(s_lsd, n)
                    for i in range(2):
                        ins = mm(lvar[:], onesk[:], lq[:, i, :], start=(i == 0), stop=(i == 1))
                    ins.then_inc(s_var, 1)
                if kind == "pw":
                    pe.wait_ge(s_twl, 2)
                    pe.wait_ge(s_llo, 2 * n + 2)
                    if n:
                        pe.wait_ge(s_lye, 2 * n)
                    for m in range(2):
                        for k in range(2):
                            ins = mm3(lpo[m][:], cwh[:, 2 * k + m, :], cwl[:, 2 * k + m, :], lsh[:, k, :], lsl[:, k, :],
                                      k == 0, k == 1)
                        ins.then_inc(s_lpw, 1)
                if kind == "pmm":
                    i, c = POOL_JOBS[n]
                    pe.wait_ge(s_twl, 2)
                    pe.wait_ge(s_pdl, n + 1)
                    if n >= 2:
                        pe.wait_ge(s_pye, n - 1)
                    mm3(pmb[n % 2][:], pwh[:, i, :], pwl[:, i, :], pdh[:], pdl[:], True, True).then_inc(s_pmm, 1)
                if kind == "gmm":
                    pe.wait_ge(s_cr, 1)
                    pe.wait_ge(s_wg[n], 32)
                    pe.wait_ge(s_ev, N_CU + len(UNITS))
                    for k in range(KD):
                        ins = mm(gob[n][:], crep[:, k, :], wg[n][:, k, :], start=(k == 0), stop=(k == KD - 1))
                    ins.then_inc(s_gmm, 1)

            pe.wait_ge(s_wol, KD)
            pe.wait_ge(s_ev, N_CU + len(UNITS))
            pe.wait_ge(s_lye, 2 * NCH)
            pe.wait_ge(s_pye, 2 * NCH)
            for n, (c, i) in enumerate(TILES):
                pe.wait_ge(s_zl, KD * (c + 1))
                if n >= 3:
                    pe.wait_ge(s_ot, n - 2)
                for h in range(2):
                    hs = slice(h * CH, (h + 1) * CH)
                    for k in range(KD):
                        zs = slice(i * P, (i + 1) * P)
                        ins = mm3(ob[n % 3][h][:], zh[:, c % 2, k, zs], zl[:, c % 2, k, zs], woh[:, k, hs], wol[:, k, hs],
                                  k == 0, k == KD - 1)
                ins.then_inc(s_om, 1)


def position_tables():
    import numpy as np
    q = D // 4
    omega = (np.float32(1.0) / (np.float32(10000.0) ** (np.arange(q, dtype=np.float32) / np.float32(q)))).astype(np.float32)

    def enc(p):
        ang = p.astype(np.float32)[:, None] * omega[None, :]
        return np.concatenate([np.sin(ang), np.cos(ang)], axis=-1).astype(np.float32)
    row = enc(np.arange(SEQ) // 64).reshape(NCH, TPC, P, D // 2).transpose(0, 2, 1, 3)
    return np.ascontiguousarray(row), enc(np.arange(P) % 64)


def pool_edges():
    import numpy as np
    e = np.ones((P, 2, 2, PH), np.float32)
    for i, h, w in ((0, 0, 2), (0, 1, 4), (1, 0, 8), (1, 1, 16)):
        for t in range(PH):
            e[64 * h:64 * h + 64, i, 0, t] = w / min(w, t + w // 2)
            back = PH - t
            e[64 * h:64 * h + 64, i, 1, t] = w / min(w, back + w // 2)
    return e.reshape(P, 32)


def kernel(**inputs):
    import numpy as np
    import concourse.bacc as bacc
    from concourse import mybir as mb
    from concourse.bass_utils import run_bass_kernel_spmd

    a = {k: np.asarray(v) for k, v in inputs.items()}

    def cols(v):
        return v.reshape(-1, P).T

    c2 = np.stack([a["c"][0].reshape(KD, P), a["c_ctx"].reshape(KD, P)], axis=1).reshape(2 * KD, P).T
    par = np.concatenate([
        c2, cols(a["b_mod"][0, :2 * D]), cols(a["g_pre"][0]), cols(a["lru_ba"][0]), cols(a["lru_bx"][0]),
        cols(a["lru_lambda"][0]), cols(a["lru_conv_w"][0].reshape(4, N_LRU, P).transpose(1, 0, 2)),
        cols(a["lru_conv_b"][0]), cols(a["pool_scale"][0]),
        cols(a["conf_dw"][0].reshape(CONF_K, 2, P).transpose(1, 0, 2)), cols(a["conf_dw_b"][0]),
        cols(a["conf_ln_g"][0]), cols(a["conf_ln_b"][0]), pool_edges()], axis=1)
    gw = np.stack([a["lru_wa"][0], a["lru_wx"][0]], axis=1)
    gw = gw.reshape(2, 2, N_LRU, 2, 64, 64).transpose(2, 3, 4, 0, 1, 5).reshape(N_LRU, P, 4, 64)
    pw = a["pool_w"][0].reshape(2, 2, 64, 64).transpose(1, 2, 0, 3)
    cw = a["conf_pw"][0].reshape(2, P, 2, P).transpose(1, 0, 2, 3).reshape(P, 4, P)
    pos_row, pos_col = position_tables()
    arrays = {
        "x": a["x"][0], "ctx": a["ctx"][0], "par": par,
        "w_mod": a["w_mod"][0].reshape(KD, P, 12, 256).transpose(2, 1, 0, 3),
        "b_gate": a["b_mod"][0, 2 * D:], "g_post": a["g_post"][0],
        "w_in": a["w_in"][0].reshape(KD, P, NT_IN, P).transpose(2, 1, 0, 3),
        "gate_w": gw, "pool_w": pw, "conf_pw": cw, "w_out": a["w_out"][0],
        "pos_row": pos_row, "pos_col": pos_col,
    }
    nc = bacc.Bacc("TRN2", target_bir_lowering=False, num_devices=1)
    f32 = mb.dt.float32
    feed, args = {}, []
    for name, v in arrays.items():
        v = np.ascontiguousarray(v)
        feed[f"in_{name}"] = v
        args.append(nc.dram_tensor(f"in_{name}", v.shape, mb.dt.from_np(v.dtype), kind="ExternalInput").ap())
    for name, shape in (("u", (NT_IN, P, SEQ)), ("uc", (N_LRU, P, CTX)), ("cv", (2, P, SEQ)), ("y", (KD, P, SEQ))):
        args.append(nc.dram_tensor(f"scratch_{name}", shape, f32, kind="Internal").ap())
    args.append(nc.dram_tensor("out_0", (SEQ, D), f32, kind="ExternalOutput").ap())
    mixer_kernel(nc, *args)
    r = run_bass_kernel_spmd(nc, [feed], core_ids=[0])
    return r.results[0]["out_0"].reshape(1, SEQ, D)
```
